# Optimizing a Trainium2 kernel written in Bass

```python
import jax, jax.numpy as jnp
from jax import lax
import numpy as np

D_MODEL = 2048
BATCH = 1
SEQ = 256
DEPTH = 1

MIX_WIDTH = D_MODEL
POOL_WINDOWS = (2, 4, 8, 16)
N_POOL_GROUPS = len(POOL_WINDOWS)
POOL_WIDTH = MIX_WIDTH // 2
POOL_GROUP_DIM = POOL_WIDTH // N_POOL_GROUPS
FOURIER_WIDTH = MIX_WIDTH - POOL_WIDTH
N_FOURIER_HEADS = 4
FOURIER_HEAD_DIM = FOURIER_WIDTH // N_FOURIER_HEADS
N_EXPERT_GROUPS = 4
EXPERTS_PER_GROUP = 4
N_EXPERTS = N_EXPERT_GROUPS * EXPERTS_PER_GROUP
TOP_K_IN_GROUP = 2
EXPERT_FF = D_MODEL // 4
RMS_EPS = 1e-6

kernel_name = "hybrid_pool_fourier_hmoe_block"

def _rmsnorm(x, g):
    xf = x.astype(jnp.float32)
    y = xf * lax.rsqrt(jnp.mean(xf * xf, axis=-1, keepdims=True) + RMS_EPS)
    return (y * g.astype(jnp.float32)).astype(x.dtype)

def _multiscale_pool_minus_token(u):
    s_len = u.shape[1]
    uf = u.astype(jnp.float32)
    c = jnp.cumsum(uf, axis=1)
    c = jnp.pad(c, ((0, 0), (1, 0), (0, 0), (0, 0)))
    t = np.arange(s_len)[:, None]
    k = np.array(POOL_WINDOWS)[None, :]
    lo = np.clip(t - (k - 1) // 2, 0, s_len)
    hi = np.clip(t + k // 2 + 1, 0, s_len)
    gid = np.arange(len(POOL_WINDOWS))[None, :]
    window_sum = c[:, hi, gid, :] - c[:, lo, gid, :]
    count = jnp.asarray((hi - lo).astype(np.float32))[None, :, :, None]
    return window_sum / count - uf

def _fourier_real(u):
    f = jnp.fft.fft2(u.astype(jnp.float32), axes=(1, 3), norm="ortho")
    return jnp.real(f)

def _hier_moe(h, w_group_router, b_group_router, w_expert_router, b_expert_router,
              w_gate, w_up, w_down):
    b, s, d = h.shape
    hf = h.reshape(b * s, d)
    g_logits = jnp.dot(hf, w_group_router).astype(jnp.float32) + b_group_router.astype(jnp.float32)
    g_probs = jax.nn.softmax(g_logits, axis=-1)
    p_g, g_idx = lax.top_k(g_probs, 1)
    e_logits = jnp.dot(hf, w_expert_router).astype(jnp.float32) + b_expert_router.astype(jnp.float32)
    e_logits = e_logits.reshape(-1, N_EXPERT_GROUPS, EXPERTS_PER_GROUP)
    e_sel = jnp.take_along_axis(e_logits, g_idx[:, :, None], axis=1)[:, 0]
    top_v, top_i = lax.top_k(e_sel, TOP_K_IN_GROUP)
    w_pair = p_g * jax.nn.softmax(top_v, axis=-1)
    expert_ids = g_idx * EXPERTS_PER_GROUP + top_i
    combine = jnp.sum(jax.nn.one_hot(expert_ids, N_EXPERTS, dtype=jnp.float32)
                      * w_pair[..., None], axis=1).astype(h.dtype)
    a = jnp.einsum('nd,edf->nef', hf, w_gate)
    v = jnp.einsum('nd,edf->nef', hf, w_up)
    act = jax.nn.silu(a) * v * combine[:, :, None]
    out = jnp.einsum('nef,efd->nd', act, w_down)
    return out.reshape(b, s, d)

def setup_inputs(seed: int = 0) -> dict:
    key = jax.random.key(seed)
    ks = jax.random.split(key, 20)
    f32 = jnp.float32
    nrm = lambda k, shp, fan: jax.random.normal(k, shp, f32) * (fan ** -0.5)
    return {
        "x": jax.random.normal(ks[0], (BATCH, SEQ, D_MODEL), f32),
        "g_mix": 1.0 + 0.02 * jax.random.normal(ks[1], (D_MODEL,), f32),
        "w_in": nrm(ks[2], (D_MODEL, MIX_WIDTH), D_MODEL),
        "w_pool": nrm(ks[3], (N_POOL_GROUPS, POOL_GROUP_DIM, POOL_GROUP_DIM), POOL_GROUP_DIM),
        "pool_scale": 1.0 + 0.02 * jax.random.normal(ks[4], (POOL_WIDTH,), f32),
        "w_fourier": nrm(ks[5], (N_FOURIER_HEADS, FOURIER_HEAD_DIM, FOURIER_HEAD_DIM), FOURIER_HEAD_DIM),
        "w_out": nrm(ks[6], (MIX_WIDTH, D_MODEL), MIX_WIDTH),
        "g_ffn": 1.0 + 0.02 * jax.random.normal(ks[7], (D_MODEL,), f32),
        "w_group_router": nrm(ks[8], (D_MODEL, N_EXPERT_GROUPS), D_MODEL),
        "b_group_router": 0.01 * jax.random.normal(ks[9], (N_EXPERT_GROUPS,), f32),
        "w_expert_router": nrm(ks[10], (D_MODEL, N_EXPERTS), D_MODEL),
        "b_expert_router": 0.01 * jax.random.normal(ks[11], (N_EXPERTS,), f32),
        "w_gate": nrm(ks[12], (N_EXPERTS, D_MODEL, EXPERT_FF), D_MODEL),
        "w_up": nrm(ks[13], (N_EXPERTS, D_MODEL, EXPERT_FF), D_MODEL),
        "w_down": nrm(ks[14], (N_EXPERTS, EXPERT_FF, D_MODEL), EXPERT_FF),
        "g_final": 1.0 + 0.02 * jax.random.normal(ks[15], (D_MODEL,), f32),
    }

def reference(x, g_mix, w_in, w_pool, pool_scale, w_fourier, w_out, g_ffn,
              w_group_router, b_group_router, w_expert_router, b_expert_router,
              w_gate, w_up, w_down, g_final):
    b, s, _ = x.shape
    for _layer in range(DEPTH):
        h = _rmsnorm(x, g_mix)
        u = jnp.dot(h, w_in)
        u_pool = u[..., :POOL_WIDTH].reshape(b, s, N_POOL_GROUPS, POOL_GROUP_DIM)
        u_four = u[..., POOL_WIDTH:].reshape(b, s, N_FOURIER_HEADS, FOURIER_HEAD_DIM)
        p = _multiscale_pool_minus_token(u_pool).astype(x.dtype)
        p = jnp.einsum('bsgc,gce->bsge', p, w_pool).reshape(b, s, POOL_WIDTH) * pool_scale
        f = _fourier_real(u_four).astype(x.dtype)
        f = jnp.einsum('bshd,hde->bshe', f, w_fourier).reshape(b, s, FOURIER_WIDTH)
        mixed = jnp.concatenate([p, f], axis=-1)
        x = x + jnp.dot(mixed, w_out)
        h2 = _rmsnorm(x, g_ffn)
        x = x + _hier_moe(h2, w_group_router, b_group_router, w_expert_router,
                          b_expert_router, w_gate, w_up, w_down)
    return _rmsnorm(x, g_final)


_drawn_inputs = setup_inputs


def setup_inputs(seed=0):
    import zlib

    import numpy as np

    out = dict(_drawn_inputs(seed))
    spreads = {}
    factors = {'g_mix': 3.026,
     'pool_scale': 3.107,
     'g_ffn': 4.738,
     'b_group_router': 8.0,
     'b_expert_router': 15.216,
     'g_final': 7.556}
    for name, (base, spread) in spreads.items():
        noise = np.random.default_rng([zlib.crc32(name.encode()), seed]).standard_normal(out[name].shape)
        drawn = base * np.exp(spread * noise) if base else spread * noise
        out[name] = __import__('jax').numpy.asarray(drawn.astype(out[name].dtype))
    for name, factor in factors.items():
        out[name] = (out[name] * factor).astype(out[name].dtype)
    return out
```

```python
import concourse.bass as bass
from concourse import mybir
from concourse.alu_op_type import AluOpType as ALU
from contextlib import ExitStack
import numpy as np

P = 128
SEQ, D = 256, 2048
TC = SEQ // P
NB, BLK = 4, 512
KPB = BLK // P
KK = D // P
POOL_GROUPS, HEADS, HD = 4, 4, 256
HC = HD // P
WINDOWS = (2, 4, 8, 16)
GROUPS, PER_GROUP = 4, 4
EXPERTS = GROUPS * PER_GROUP
LOGITS = GROUPS + EXPERTS
FF = 512
FC = FF // P
CAP = 64
PAIRS = EXPERTS // 2
EPS = 1e-6
SLOTS = 12
LOOP_SLOTS = 8
SLOT = KPB * BLK
PAIR_SLABS = 2 * 3 * KPB
HALF = SLOT // 2
FAR = 1.0e30

C_ID, C_TRI, C_ONES, C_IOTA, C_IDX = 0, P, 2 * P, 3 * P, 3 * P + CAP
C_FULL = C_IDX + EXPERTS
MAX_ROUNDS = SEQ // CAP
C_WIDTH = C_FULL + MAX_ROUNDS - 1


def build(nc, x, g_mix, w_in, w_pool, pool_scale, w_fourier, w_out, g_ffn, w_group_router,
          b_group_router, w_expert_router, b_expert_router, w_gate, w_up, w_down, g_final,
          consts, dft_tokens, dft_channels, pool_windows, out):
    f32, f32r, i32 = mybir.dt.float32, mybir.dt.float32r, mybir.dt.int32
    ACT = mybir.ActivationFunctionType
    AX = mybir.AxisListType

    ctx = ExitStack()
    with ctx:
        def sem(name):
            return ctx.enter_context(nc.semaphore(name))

        def sb(name, shape, dt=f32, where=ctx):
            return where.enter_context(nc.sbuf_tensor(name, shape, dt))

        ring = sb("ring", [P, SLOTS, SLOT])
        xs = sb("xs", [P, TC, D])
        u = sb("u", [P, TC, D])
        mid = sb("mid", [P, 2, HEADS, HC * SEQ])
        cst = sb("cst", [P, C_WIDTH])
        group_w = sb("group_w", [P, NB, KPB * GROUPS])
        expert_w = sb("expert_w", [P, NB, KPB * EXPERTS])
        router_w = sb("router_w", [P, KK, LOGITS])
        gmix = sb("gmix", [P, KK])
        gffn = sb("gffn", [P, KK])
        pscale = sb("pscale", [P, POOL_GROUPS * HC])
        bias = sb("bias", [P, LOGITS])
        ssq = sb("ssq", [P, TC, NB])
        rms = sb("rms", [P, TC])
        rinv = sb("rinv", [P, TC])
        rinv2 = sb("rinv2", [P, TC])
        logit_sum = sb("logit_sum", [P, TC, LOGITS])
        sel = sb("sel", [P, TC, EXPERTS])
        comb = sb("comb", [P, TC, EXPERTS])
        rank = sb("rank", [P, TC, EXPERTS])
        rounds = sb("rounds", [P, 1], i32)
        junk = sb("junk", [P, BLK])
        logit = sb("logit", [P, TC, LOGITS])
        hit = sb("hit", [P, TC, EXPERTS])
        first_group = sb("first_group", [P, TC, GROUPS])
        masked = sb("masked", [P, TC, EXPERTS])
        masked2 = sb("masked2", [P, TC, EXPERTS])
        best = sb("best", [P, TC, EXPERTS])
        second = sb("second", [P, TC, EXPERTS])
        top = sb("top", [P, 4, TC])
        to_exp = sb("to_exp", [P, TC, GROUPS + 1])
        exps = sb("exps", [P, TC, GROUPS + 1])
        share = sb("share", [P, 4, TC])
        over = sb("over", [P, MAX_ROUNDS])
        fullest = sb("fullest", [P, 1])
        pair_rank = sb("pair_rank", [P, TC, 2])
        pair_comb = sb("pair_comb", [P, TC, 2])

        early = ExitStack()
        tr_hi = sb("tr_hi", [P, KK, SEQ], f32r, early)
        tr_lo = sb("tr_lo", [P, KK, SEQ], f32r, early)
        w_hi = sb("w_hi", [P, 2, HALF], f32r, early)
        w_lo = sb("w_lo", [P, 2, HALF], f32r, early)
        early.close()
        picked = sb("picked", [P, KK, 2 * CAP])
        expert_out = sb("expert_out", [2 * CAP, D])
        silu = sb("silu", [2 * CAP, FF])
        act_rows = sb("act_rows", [2 * CAP, FF])
        act_cols = sb("act_cols", [P, FC, 2 * CAP])
        pick = sb("pick", [P, TC, 2 * CAP])
        put = sb("put", [P, TC, 2 * CAP])
        put_t = sb("put_t", [2 * CAP, SEQ])
        gfin = sb("gfin", [P, D])

        bank = [ctx.enter_context(nc.psum_tensor(f"bank{i}", [P, BLK], f32)) for i in range(8)]

        ident, tri = cst[:, C_ID:C_ID + P], cst[:, C_TRI:C_TRI + P]
        bound = cst[:, C_FULL:C_FULL + MAX_ROUNDS - 1]
        ones, iota = cst[:, C_ONES:C_ONES + P], cst[:, C_IOTA:C_IOTA + CAP]
        index = cst[:, C_IDX:C_IDX + EXPERTS]
        stage = mid[:, 0].rearrange("p h n -> p (h n)")[:, :4 * BLK].rearrange(
            "p (b t k c) -> p b t k c", b=2, t=TC, k=KPB)
        x2t = mid[:, 1].rearrange("p h n -> p (h n)")[:, :4 * BLK].rearrange(
            "p (b t k c) -> p b t k c", b=2, t=TC, k=KPB)
        snap = u[:, :, :].rearrange("p t (k c) -> p t k c", k=KK)
        ab, pooled = mid[:, 0], mid[:, 1]
        pq = u[:, 0, :].rearrange("p (h n) -> p h n", h=HEADS)
        real = u[:, 1, :].rearrange("p (h n) -> p h n", h=HEADS)

        AHEAD = 1
        slot_full = [sem(f"slot_full{i}") for i in range(SLOTS)]
        slot_free = [sem(f"slot_free{i}") for i in range(SLOTS)]
        x_in = [sem(f"x_in{i}") for i in range(NB)]
        small_in = sem("small_in")
        gfin_in = sem("gfin_in")
        x_turned = sem("x_turned")
        h_hi = sem("h_hi")
        h_lo = sem("h_lo")
        squares = sem("squares")
        mean_ready = sem("mean_ready")
        root_ready = sem("root_ready")
        rinv_ready = sem("rinv_ready")
        hi_ready = sem("hi_ready")
        lo_ready = sem("lo_ready")
        half_used = sem("half_used")
        u_out = [sem(f"u_out{i}") for i in range(2)]
        unit_done = sem("unit_done")
        unit_act = sem("unit_act")
        unit_dve = sem("unit_dve")
        router_scaled = sem("router_scaled")
        staged = sem("staged")
        x2_out = [sem(f"x2_out{i}") for i in range(2)]
        x2_turned = sem("x2_turned")
        x2t_out = sem("x2t_out")
        snapped = sem("snapped")
        logits_done = sem("logits_done")
        logits_out = sem("logits_out")
        step = sem("step")
        exp_ready = sem("exp_ready")
        exp_asked = sem("exp_asked")
        sel_ready = sem("sel_ready")
        ranks_done = sem("ranks_done")
        rounds_ready = sem("rounds_ready")
        zeroed = sem("zeroed")
        pair_cols = sem("pair_cols")
        pick_ready = sem("pick_ready")
        rank_moved = sem("rank_moved")
        swap_full = sem("swap_full")
        swap_free = [sem(f"swap_free{i}") for i in range(2)]
        silu_ready = sem("silu_ready")
        act_ready = sem("act_ready")
        down_out = sem("down_out")
        last_squares = sem("last_squares")
        last_mean = sem("last_mean")
        last_root = sem("last_root")
        last_rinv = sem("last_rinv")
        y_ready = sem("y_ready")
        out_done = sem("out_done")

        w_in_v = w_in.rearrange("(g p k) (i b n) -> g p k i b n", p=P, k=KPB, i=2, b=2)
        w_out_v = w_out.rearrange("(g k p) (i b n) -> g p k i b n", p=P, k=KPB, i=2, b=2)
        gate_v = w_gate.rearrange("(q e) (g p k) n -> q e g p (k n)", e=2, p=P, k=KPB)
        up_v = w_up.rearrange("(q e) (g p k) n -> q e g p (k n)", e=2, p=P, k=KPB)
        down_v = w_down.rearrange("(q e) (c p) n -> q e c p n", e=2, p=P)

        HALVES = 2 * LOOP_SLOTS
        TURNS = NB // 2
        U_AB, U_MEAN, U_PQ, U_WP, U_WF, UNITS = 0, 4, 8, 12, 16, 20
        SWAPS = 14
        N_COS = SEQ // 2 + 1

        def slot_of(j):
            return (j + LOOP_SLOTS) % SLOTS

        LOADED = [16 * 2 * TURNS] * LOOP_SLOTS + [32, 16, 16, 16]
        GATE_UP_LAST, DOWN_LAST = slot_of(4 * NB - 1), slot_of(PAIR_SLABS - 1)

        block = ctx.enter_context(nc.Block())

        @block.sync
        def _(sp):
            for ahead in slot_free:
                sp.sem_inc(ahead, AHEAD)
            for g in range(NB):
                sp.dma_start(xs[:, :, g * BLK:(g + 1) * BLK],
                             x.rearrange("(t p) n -> p t n", p=P)[:, :, g * BLK:(g + 1) * BLK]).then_inc(x_in[g], 16)

            def load_slab(w, i, j):
                b, g = divmod(j, NB)
                sp.dma_start(ring[:, j].rearrange("p (k n) -> p k n", k=KPB),
                             w[g][:, :, i, b, :]).then_inc(slot_full[j], 16)

            for i in range(TURNS):
                for j in range(LOOP_SLOTS):
                    if i:
                        sp.wait_ge(lo_ready, (i - 1) * HALVES + 2 * j + 2)
                    load_slab(w_in_v, i, j)
            for slot, at, view in ((8, 0, dft_tokens.rearrange("(s p) n -> p s n", p=P)),
                                   (8, TC * SEQ, dft_channels.rearrange("(s p) n -> p s n", p=P)),
                                   (9, 0, pool_windows.rearrange("(s p) n -> p s n", p=P)),
                                   (10, 0, w_pool.rearrange("g (s p) n -> p (g s) n", p=P)),
                                   (11, 0, w_fourier.rearrange("g (s p) n -> p (g s) n", p=P))):
                n = view.shape[1] * view.shape[2]
                sp.dma_start(ring[:, slot, at:at + n].rearrange("p (k n) -> p k n", k=view.shape[1]),
                             view).then_inc(slot_full[slot], 16)
            for i in range(TURNS):
                for j in range(LOOP_SLOTS):
                    sp.wait_ge(lo_ready, (TURNS - 1 + i) * HALVES + 2 * j + 2)
                    load_slab(w_out_v, i, j)
            sp.wait_ge(unit_done, UNITS)

            def experts(q, turn):
                for j in range(PAIR_SLABS):
                    s = slot_of(j)
                    if j < 4 * NB:
                        e, w = j % 2, (gate_v, up_v)[j % 4 // 2]
                        src = w[bass.ds(q, 1), e, j // 4]
                    else:
                        src = down_v[bass.ds(q, 1), j % 2, (j - 4 * NB) // 2]
                    if j < SLOTS and s < LOOP_SLOTS:
                        sp.wait_ge(lo_ready, (2 * TURNS - 1) * HALVES + 2 * s + 2)
                    sp.wait_ge(slot_free[s], AHEAD + turn * 2 + j // SLOTS)
                    sp.dma_start(ring[:, s], src.rearrange("q p n -> p (q n)")).then_inc(slot_full[s], 16)

            with sp.Fori(0, PAIRS) as q:
                experts(q, q)
            sp.wait_ge(rounds_ready, 1)
            more = sp.value_load(rounds[0:1, 0:1], min_val=1, max_val=MAX_ROUNDS)
            with sp.If(more > 1):
                with sp.Fori(1, more) as r:
                    with sp.Fori(0, PAIRS) as q:
                        experts(q, r * PAIRS + q)
            for i in range(4):
                t, half = divmod(i, 2)
                sp.wait_ge(y_ready, i + 1)
                sp.dma_start(out[t * P:(t + 1) * P, half * D // 2:(half + 1) * D // 2],
                             xs[:, t, half * D // 2:(half + 1) * D // 2]).then_inc(out_done, 16)
            sp.wait_ge(out_done, 64)

        @block.tensor
        def _(pe):
            for ahead in (*u_out, *x2_out, *swap_free, x2t_out, logits_out, down_out):
                pe.sem_inc(ahead, AHEAD)
            pe.sem_inc(half_used, AHEAD + 1)
            pe.wait_ge(small_in, 16 * 8)
            for g in range(NB):
                pe.wait_ge(x_in[g], 16)
                if g >= 2:
                    pe.wait_ge(h_lo, KPB * (g - 1))
                for k in range(KPB):
                    for t in range(TC):
                        src = xs[:, t, g * BLK:(g + 1) * BLK].rearrange("p (c k) -> p k c", k=KPB)[:, k]
                        dst = bank[4 + (g % 2) * 2 + k // 2][:, (k % 2) * SEQ + t * P:(k % 2) * SEQ + (t + 1) * P]
                        last = nc.tensor.transpose(dst, src, ident)
                last.then_inc(x_turned, 1)

            def half_products(b, g, h, turn, before):
                pe.wait_ge(lo_ready, turn * HALVES + before + (b * NB + g) * 2 + h + 1)
                for kl in range(2):
                    kk = g * KPB + h * 2 + kl
                    for t in range(TC):
                        dst = bank[2 * b + t][:, :]
                        hi_t, lo_t = (m[:, kk, t * P:(t + 1) * P] for m in (tr_hi, tr_lo))
                        hi_w, lo_w = (m[:, h, kl * BLK:(kl + 1) * BLK] for m in (w_hi, w_lo))
                        nc.tensor.matmul(dst, hi_t, hi_w, start=kk == 0, stop=False)
                        nc.tensor.matmul(dst, hi_t, lo_w, start=False, stop=False)
                        last = nc.tensor.matmul(dst, lo_t, hi_w, start=False, stop=kk == KK - 1)
                last.then_inc(half_used, 1)

            pe.wait_ge(h_lo, KK)
            with pe.Fori(0, TURNS) as turn:
                for b in range(2):
                    pe.wait_ge(u_out[b], AHEAD + 2 * turn)
                    for g in range(NB):
                        for h in range(2):
                            half_products(b, g, h, turn, 0)

            for b in range(2):
                pe.wait_ge(u_out[b], AHEAD + 2 * TURNS)
            pe.wait_ge(slot_full[8], 32)
            for h in range(HEADS):
                for c in range(HC):
                    for s in range(TC):
                        col = D // 2 + h * HD + c * P
                        last = nc.tensor.matmul(bank[h][:, c * SEQ:(c + 1) * SEQ], u[:, s, col:col + P],
                                                ring[:, 8, s * SEQ:(s + 1) * SEQ], start=s == 0, stop=s == TC - 1)
                last.then_inc(unit_done, 1)
            pe.wait_ge(slot_full[9], 16)
            for g in range(POOL_GROUPS):
                for c in range(HC):
                    for s in range(TC):
                        col = g * HD + c * P
                        last = nc.tensor.matmul(bank[4 + g][:, c * SEQ:(c + 1) * SEQ], u[:, s, col:col + P],
                                                ring[:, 9, (g * TC + s) * SEQ:(g * TC + s + 1) * SEQ],
                                                start=s == 0, stop=s == TC - 1)
                last.then_inc(unit_done, 1)
            for h in range(HEADS):
                pe.wait_ge(unit_act, h + 1)
                for c in range(HC):
                    for part, (a, b) in enumerate(((0, N_COS), (N_COS, SEQ))):
                        for s in range(HC):
                            wcol = TC * SEQ + (part * HC + s) * HD + c * P
                            last = nc.tensor.matmul(bank[h][:, c * SEQ + a:c * SEQ + b], ring[:, 8, wcol:wcol + P],
                                                    ab[:, h, s * SEQ + a:s * SEQ + b],
                                                    start=s == 0, stop=s == HC - 1)
                last.then_inc(unit_done, 1)
            pe.wait_ge(slot_full[10], 16)
            for g in range(POOL_GROUPS):
                pe.wait_ge(unit_dve, g + 1)
                for e in range(HC):
                    for c in range(HC):
                        wcol = (g * HC + c) * HD + e * P
                        last = nc.tensor.matmul(bank[4 + g][:, e * SEQ:(e + 1) * SEQ], ring[:, 10, wcol:wcol + P],
                                                pooled[:, g, c * SEQ:(c + 1) * SEQ], start=c == 0, stop=c == HC - 1)
                last.then_inc(unit_done, 1)
            pe.wait_ge(slot_full[11], 16)
            for h in range(HEADS):
                pe.wait_ge(unit_dve, POOL_GROUPS + h + 1)
                for e in range(HC):
                    for c in range(HC):
                        wcol = (h * HC + c) * HD + e * P
                        last = nc.tensor.matmul(bank[h][:, e * SEQ:(e + 1) * SEQ], ring[:, 11, wcol:wcol + P],
                                                real[:, h, c * SEQ:(c + 1) * SEQ], start=c == 0, stop=c == HC - 1)
                last.then_inc(unit_done, 1)

            def turn_x2(b, turn):
                pe.wait_ge(staged, turn * 4 + 2 * b + 2)
                pe.wait_ge(x2t_out, AHEAD + turn * 4 + 2 * b)
                for t in range(TC):
                    for k in range(KPB):
                        last = nc.tensor.transpose(bank[4 + t][:, k * P:(k + 1) * P], stage[:, b, t, k], ident)
                last.then_inc(x2_turned, 1)

            def logit_products(b, turn):
                pe.wait_ge(x2t_out, AHEAD + turn * 4 + 2 * b + 2)
                if b == 0:
                    pe.wait_ge(logits_out, AHEAD + turn)
                for t in range(TC):
                    for k in range(KPB):
                        w = router_w[:, bass.ds((turn * 2 + b) * KPB + k, 1), :].rearrange("p a n -> p (a n)")
                        last = nc.tensor.matmul(bank[6 + t][:, 0:LOGITS], x2t[:, b, t, k], w,
                                                start=b == 0 and k == 0, stop=b == 1 and k == KPB - 1)
                if b == 1:
                    last.then_inc(logits_done, 1)

            pe.wait_ge(unit_dve, 4 * HEADS)
            pe.wait_ge(router_scaled, 1)
            with pe.Fori(0, TURNS) as turn:
                for b in range(2):
                    pe.wait_ge(x2_out[b], AHEAD + 2 * turn)
                    for g in range(NB):
                        for h in range(2):
                            half_products(b, g, h, turn, TURNS * HALVES)
                        if b == 1 and g == 0:
                            turn_x2(0, turn)
                        if b == 1 and g == 1:
                            logit_products(0, turn)
                turn_x2(1, turn)
                logit_products(1, turn)

            pe.wait_ge(sel_ready, 1)
            pe.wait_ge(logits_out, AHEAD + TURNS)
            for col, parts in ((0, ((tri, 0),)), (1, ((ones, 0), (tri, 1))), (2, ((ones, 0), (ones, 1)))):
                for i, (m, t) in enumerate(parts):
                    last = nc.tensor.matmul(bank[6][:, col * EXPERTS:(col + 1) * EXPERTS], m, sel[:, t],
                                            start=i == 0, stop=i == len(parts) - 1)
            last.then_inc(ranks_done, 1)

            pe.wait_ge(rounds_ready, 1)
            more = pe.value_load(rounds[0:1, 0:1], min_val=1, max_val=MAX_ROUNDS)
            pe.wait_ge(snapped, AHEAD + 2 * NB)
            pe.wait_ge(zeroed, 2)

            def scatter(turn, first):
                pe.wait_ge(down_out, AHEAD + turn)
                for j in range(TC * NB):
                    t, n = divmod(j, NB)
                    use = first + j
                    pe.wait_ge(swap_free[use % 2], AHEAD + turn * (SWAPS // 2) + use // 2)
                    nc.tensor.matmul(bank[6 + use % 2][:, :], put_t[:, t * P:(t + 1) * P],
                                     expert_out[:, n * BLK:(n + 1) * BLK], start=True, stop=True).then_inc(swap_full, 1)

            def slab_in(j, turn):
                pe.wait_ge(slot_full[slot_of(j)], turn * 32 + LOADED[slot_of(j)] + 16 * (j // SLOTS + 1))

            def pair(turn):
                pe.wait_ge(pick_ready, turn + 1)
                for g in range(NB):
                    pe.wait_ge(swap_free[g % 2], AHEAD + turn * (SWAPS // 2) + g // 2)
                    for k in range(KPB):
                        for t in range(TC):
                            last = nc.tensor.matmul(bank[6 + g % 2][:, k * P:(k + 1) * P], snap[:, t, g * KPB + k],
                                                    pick[:, t], start=t == 0, stop=t == TC - 1)
                    last.then_inc(swap_full, 1)
                for g in range(NB):
                    for j in range(4):
                        slab_in(4 * g + j, turn)
                    pe.wait_ge(swap_free[g % 2], AHEAD + turn * (SWAPS // 2) + g // 2 + 1)
                    for k in range(KPB):
                        kk = g * KPB + k
                        for j in range(4):
                            e, which = j % 2, j // 2
                            s = slot_of(4 * g + j)
                            last = nc.tensor.matmul(bank[which][e * CAP:(e + 1) * CAP, :],
                                                    picked[:, kk, e * CAP:(e + 1) * CAP],
                                                    ring[:, s, k * BLK:(k + 1) * BLK],
                                                    start=kk == 0, stop=kk == KK - 1)
                            if k == KPB - 1:
                                last.then_inc(slot_free[s], 1)
                scatter(turn, 4)
                pe.wait_ge(swap_free[0], AHEAD + turn * (SWAPS // 2) + 6)
                for t in range(TC):
                    last = nc.tensor.transpose(bank[6][:, t * P:(t + 1) * P], put[:, t], ident)
                last.then_inc(swap_full, 1)
                pe.wait_ge(act_ready, turn + 1)
                pe.wait_ge(swap_free[1], AHEAD + turn * (SWAPS // 2) + 6)
                for c in range(FC):
                    last = nc.tensor.transpose(bank[7][:, c * P:(c + 1) * P], act_rows[:, c * P:(c + 1) * P], ident)
                last.then_inc(swap_full, 1)
                pe.wait_ge(swap_free[1], AHEAD + turn * (SWAPS // 2) + 7)
                for c in range(FC):
                    for e in range(2):
                        slab_in(4 * NB + 2 * c + e, turn)
                    for n in range(NB):
                        for e in range(2):
                            s = slot_of(4 * NB + 2 * c + e)
                            last = nc.tensor.matmul(bank[2 + n][e * CAP:(e + 1) * CAP, :],
                                                    act_cols[:, c, e * CAP:(e + 1) * CAP],
                                                    ring[:, s, n * BLK:(n + 1) * BLK],
                                                    start=c == 0, stop=c == FC - 1)
                            if n == NB - 1:
                                last.then_inc(slot_free[s], 1)

            with pe.Fori(0, more) as r:
                with pe.Fori(0, PAIRS) as q:
                    pair(r * PAIRS + q)
            scatter(more * PAIRS, 0)

        @block.scalar
        def _(act):
            act.sem_inc(snapped, AHEAD)
            act.dma_start(cst[:], consts).then_inc(small_in, 16)
            for dst, g in ((gmix, g_mix), (gffn, g_ffn)):
                act.dma_start(dst[:].rearrange("p (g k) -> p g k", k=KPB),
                              g.rearrange("(g p k) -> p g k", p=P, k=KPB)).then_inc(small_in, 16)
            with nc.allow_non_contiguous_dma(reason="eight scalars of a partition"):
                act.dma_start(pscale[:], pool_scale.rearrange("(c p) -> p c", p=P)).then_inc(small_in, 16)
            for dst, w in ((group_w, w_group_router), (expert_w, w_expert_router)):
                act.dma_start(dst[:], w.rearrange("(g p k) n -> p g (k n)", p=P, k=KPB)).then_inc(small_in, 16)
            for first, n, b in ((0, GROUPS, b_group_router), (GROUPS, EXPERTS, b_expert_router)):
                act.dma_start(bias[:, first:first + n], b.unsqueeze(0).to_broadcast([P, n])).then_inc(small_in, 16)

            act.wait_ge(small_in, 16 * 8)
            for g in range(NB):
                act.wait_ge(x_turned, g + 1)
                for k in range(KPB):
                    kk = g * KPB + k
                    src = bank[4 + (g % 2) * 2 + k // 2][:, (k % 2) * SEQ:(k % 2 + 1) * SEQ]
                    nc.scalar.mul(tr_hi[:, kk], src, gmix[:, kk:kk + 1]).then_inc(h_hi, 1)

            def high_part(j, h, turn, before):
                if h == 0:
                    act.wait_ge(slot_full[j], turn * 16 + before // HALVES * 16 + 16)
                act.wait_ge(half_used, AHEAD + turn * HALVES + before + 2 * j + h)
                nc.scalar.copy(w_hi[:, h], ring[:, j, h * HALF:(h + 1) * HALF]).then_inc(hi_ready, 1)

            for t in range(TC):
                last = nc.scalar.activation(mid[:, t].rearrange("p h n -> p (h n)"), xs[:, t], ACT.Square,
                                            accum_out=ssq[:, t, 0:1])
            last.then_inc(squares, 1)
            act.wait_ge(mean_ready, 1)
            nc.scalar.activation(rms[:], rms[:], ACT.Sqrt).then_inc(root_ready, 1)

            act.wait_ge(rinv_ready, 1)
            with act.Fori(0, TURNS) as turn:
                def u_block(b):
                    act.wait_ge(half_used, AHEAD + turn * HALVES + NB * 2 * (b + 1) + 1)
                    nc.scalar.mul(u[:, 0, bass.ds((turn * 2 + b) * BLK, BLK)], bank[2 * b][:, :],
                                  rinv[:, 0:1]).then_inc(u_out[b], 1)
                for j in range(LOOP_SLOTS):
                    for h in range(2):
                        high_part(j, h, turn, 0)
                    if j == NB:
                        u_block(0)
                u_block(1)

            for h in range(HEADS):
                act.wait_ge(unit_done, U_AB + h + 1)
                nc.scalar.copy(ab[:, h], bank[h][:, :]).then_inc(unit_act, 1)
            for h in range(HEADS):
                act.wait_ge(unit_done, U_PQ + h + 1)
                nc.scalar.copy(pq[:, h], bank[h][:, :]).then_inc(unit_act, 1)
            for g in range(POOL_GROUPS):
                act.wait_ge(unit_done, U_WP + g + 1)
                for e in range(HC):
                    m = g * HC + e
                    last = nc.scalar.mul(tr_hi[:, m], bank[4 + g][:, e * SEQ:(e + 1) * SEQ], pscale[:, m:m + 1])
                last.then_inc(unit_act, 1)
            for h in range(HEADS):
                act.wait_ge(unit_done, U_WF + h + 1)
                m = (POOL_GROUPS + h) * HC
                nc.scalar.copy(tr_hi[:, m:m + HC].rearrange("p c n -> p (c n)"), bank[h][:, :]).then_inc(unit_act, 1)

            with act.Fori(0, TURNS) as turn:
                def turned_block(b):
                    act.wait_ge(x2_turned, AHEAD + turn * 2 + b + 1)
                    for t in range(TC):
                        nc.scalar.copy(x2t[:, b, t].rearrange("p k c -> p (k c)"), bank[4 + t][:, :]).then_inc(x2t_out, 1)

                def snapshot(b):
                    for t in range(TC):
                        act.wait_ge(staged, turn * 4 + 2 * b + t + 1)
                        nc.scalar.copy(snap[:, t, bass.ds((turn * 2 + b) * KPB, KPB), :], stage[:, b, t])
                        act.wait_ge(snapped, AHEAD + turn * 4 + 2 * b + t)
                        nc.scalar.activation(junk[:], stage[:, b, t].rearrange("p k c -> p (k c)"), ACT.Square,
                                             accum_out=ssq[:, t, bass.ds(turn * 2 + b, 1)]).then_inc(snapped, 1)
                for j in range(LOOP_SLOTS):
                    for h in range(2):
                        high_part(j, h, turn, TURNS * HALVES)
                    if j == NB + 1:
                        turned_block(0)
                    if j == NB + 2:
                        snapshot(0)
                turned_block(1)
                snapshot(1)

            act.wait_ge(half_used, AHEAD + 2 * TURNS * HALVES + 1)
            act.dma_start(gfin[:], g_final.unsqueeze(0).to_broadcast([P, D])).then_inc(gfin_in, 16)

            act.wait_ge(exp_asked, 1)
            nc.scalar.activation(rms[:], rms[:], ACT.Sqrt).then_inc(exp_ready, 1)
            act.wait_ge(exp_asked, 2)
            nc.scalar.activation(exps[:], to_exp[:], ACT.Exp).then_inc(exp_ready, 1)

            act.wait_ge(rounds_ready, 1)
            more = act.value_load(rounds[0:1, 0:1], min_val=1, max_val=MAX_ROUNDS)

            def pair(turn):
                for g in (1, 3):
                    act.wait_ge(swap_full, turn * SWAPS + g + 1)
                    for k in range(KPB):
                        kk = g * KPB + k
                        last = nc.scalar.mul(picked[:, kk], bank[7][:, k * P:(k + 1) * P], gffn[:, kk:kk + 1])
                    last.then_inc(swap_free[1], 1)
                act.wait_ge(slot_free[GATE_UP_LAST], AHEAD + turn * 2 + 2)
                nc.scalar.activation(silu[:], bank[0][:, :], ACT.Silu).then_inc(silu_ready, 1)
                act.wait_ge(swap_full, turn * SWAPS + SWAPS)
                nc.scalar.copy(act_cols[:].rearrange("p c n -> p (c n)"), bank[7][:, :]).then_inc(swap_free[1], 1)
                act.wait_ge(slot_free[DOWN_LAST], AHEAD + turn * 2 + 2)
                for n in range(NB):
                    last = nc.scalar.copy(expert_out[:, n * BLK:(n + 1) * BLK], bank[2 + n][:, :])
                last.then_inc(down_out, 1)

            with act.Fori(0, more) as r:
                with act.Fori(0, PAIRS) as q:
                    pair(r * PAIRS + q)

            done = more * PAIRS
            for t in range(TC):
                for i in range(2):
                    act.wait_ge(swap_free[i], AHEAD + done * (SWAPS // 2) + 2 * (t + 1))
                nc.scalar.activation(expert_out[:], xs[:, t], ACT.Square, accum_out=ssq[:, t, 0:1]).then_inc(last_squares, 1) \
                    if t else nc.scalar.activation(u[:, 0], xs[:, t], ACT.Square, accum_out=ssq[:, t, 0:1]).then_inc(last_squares, 1)
                act.wait_ge(last_mean, t + 1)
                nc.scalar.activation(rms[:, t:t + 1], rms[:, t:t + 1], ACT.Sqrt).then_inc(last_root, 1)

        @block.gpsimd
        def _(pool):
            pool.wait_ge(half_used, AHEAD + 2 * TURNS * HALVES + 1)
            nc.gpsimd.memset(expert_out[:], 0.0).then_inc(zeroed, 1)
            nc.gpsimd.memset(put_t[:], 0.0).then_inc(zeroed, 1)

        @block.vector
        def _(dve):
            dve.sem_inc(x2_turned, AHEAD)
            dve.sem_inc(rank_moved, AHEAD)
            steps = [0]

            def link(instruction):
                steps[0] += 1
                instruction.then_inc(step, 1)
                dve.wait_ge(step, steps[0])

            dve.wait_ge(small_in, 16 * 8)
            for g in range(NB):
                for k in range(KPB):
                    kk = g * KPB + k
                    dve.wait_ge(h_hi, (kk // 2 + 1) * 2)
                    src = bank[4 + (g % 2) * 2 + k // 2][:, (k % 2) * SEQ:(k % 2 + 1) * SEQ]
                    nc.vector.scalar_tensor_tensor(out=tr_lo[:, kk], in0=src, scalar=gmix[:, kk:kk + 1],
                                                   in1=tr_hi[:, kk].bitcast(f32), op0=ALU.mult,
                                                   op1=ALU.subtract).then_inc(h_lo, 1)
            nc.vector.memset(logit_sum[:], 0.0)
            for w, first, n in ((group_w, 0, GROUPS), (expert_w, GROUPS, EXPERTS)):
                last = nc.vector.tensor_tensor(router_w[:, :, first:first + n],
                                               w[:].rearrange("p g (k n) -> p (g k) n", n=n),
                                               gffn[:].unsqueeze(2).to_broadcast([P, KK, n]), ALU.mult)
            last.then_inc(router_scaled, 1)
            dve.wait_ge(squares, 1)
            nc.vector.tensor_scalar(rms[:], ssq[:, :, 0], 1.0 / D, EPS, ALU.mult, ALU.add).then_inc(mean_ready, 1)
            dve.wait_ge(root_ready, 1)
            nc.vector.reciprocal(rinv[:], rms[:]).then_inc(rinv_ready, 1)
            dve.wait_ge(rinv_ready, 1)

            def low_part(j, h, turn, before):
                dve.wait_ge(hi_ready, turn * HALVES + before + 2 * j + h + 1)
                nc.vector.tensor_tensor(w_lo[:, h], ring[:, j, h * HALF:(h + 1) * HALF], w_hi[:, h].bitcast(f32),
                                        ALU.subtract).then_inc(lo_ready, 1)

            with dve.Fori(0, TURNS) as turn:
                def u_block(b):
                    dve.wait_ge(half_used, AHEAD + turn * HALVES + NB * 2 * (b + 1) + 1)
                    nc.vector.tensor_scalar(u[:, 1, bass.ds((turn * 2 + b) * BLK, BLK)], bank[2 * b + 1][:, :],
                                            rinv[:, 1:2], None, ALU.mult).then_inc(u_out[b], 1)
                for j in range(LOOP_SLOTS):
                    for h in range(2):
                        low_part(j, h, turn, 0)
                    if j == NB:
                        u_block(0)
                u_block(1)

            for g in range(POOL_GROUPS):
                dve.wait_ge(unit_done, U_MEAN + g + 1)
                nc.vector.tensor_copy(pooled[:, g], bank[4 + g][:, :]).then_inc(unit_dve, 1)
            for h in range(HEADS):
                dve.wait_ge(unit_act, HEADS + h + 1)
                both = pq[:, h].rearrange("p (c n) -> p c n", c=HC)
                to = real[:, h].rearrange("p (c n) -> p c n", c=HC)
                mid_k = SEQ // 2
                nc.vector.tensor_copy(to[:, :, 0:mid_k + 1:mid_k], both[:, :, 0:mid_k + 1:mid_k])
                nc.vector.tensor_tensor(to[:, :, 1:mid_k], both[:, :, 1:mid_k], both[:, :, N_COS:SEQ], ALU.subtract)
                nc.vector.tensor_tensor(to[:, :, SEQ - 1:mid_k:-1], both[:, :, 1:mid_k], both[:, :, N_COS:SEQ],
                                        ALU.add).then_inc(unit_dve, 1)
            for g in range(POOL_GROUPS):
                dve.wait_ge(unit_act, 2 * HEADS + g + 1)
                for e in range(HC):
                    m = g * HC + e
                    last = nc.vector.scalar_tensor_tensor(out=tr_lo[:, m], in0=bank[4 + g][:, e * SEQ:(e + 1) * SEQ],
                                                          scalar=pscale[:, m:m + 1], in1=tr_hi[:, m].bitcast(f32),
                                                          op0=ALU.mult, op1=ALU.subtract)
                last.then_inc(unit_dve, 1)
            for h in range(HEADS):
                dve.wait_ge(unit_act, 3 * HEADS + h + 1)
                m = (POOL_GROUPS + h) * HC
                nc.vector.tensor_tensor(tr_lo[:, m:m + HC].rearrange("p c n -> p (c n)"), bank[h][:, :],
                                        tr_hi[:, m:m + HC].rearrange("p c n -> p (c n)").bitcast(f32),
                                        ALU.subtract).then_inc(unit_dve, 1)

            with dve.Fori(0, TURNS) as turn:
                def x2_block(b):
                    dve.wait_ge(half_used, AHEAD + TURNS * HALVES + turn * HALVES + NB * 2 * (b + 1) + 1)
                    dve.wait_ge(snapped, AHEAD + turn * 4)
                    dve.wait_ge(x2_turned, AHEAD + turn * 2)
                    for t in range(TC):
                        cols = xs[:, t, bass.ds((turn * 2 + b) * BLK, BLK)]
                        nc.vector.tensor_tensor(cols, bank[2 * b + t][:, :], cols, ALU.add).then_inc(x2_out[b], 1)
                    dve.wait_ge(x2_out[b], AHEAD + turn * 2 + 2)
                    for t in range(TC):
                        cols = xs[:, t, bass.ds((turn * 2 + b) * BLK, BLK)]
                        nc.vector.tensor_scalar(stage[:, b, t], cols.rearrange("p (c k) -> p k c", k=KPB), 1.0, None,
                                                ALU.mult).then_inc(staged, 1)
                for j in range(LOOP_SLOTS):
                    for h in range(2):
                        low_part(j, h, turn, TURNS * HALVES)
                    if j == NB:
                        x2_block(0)
                x2_block(1)
                dve.wait_ge(logits_done, turn + 1)
                dve.wait_ge(logits_out, AHEAD + turn)
                for t in range(TC):
                    last = nc.vector.tensor_tensor(logit_sum[:, t], bank[6 + t][:, 0:LOGITS], logit_sum[:, t], ALU.add)
                last.then_inc(logits_out, 1)

            def wide(row, n):
                return row.unsqueeze(2).to_broadcast([P, TC, n])

            def first_max(values, n, row, mask):
                idx = index[:, EXPERTS - n:].unsqueeze(1).to_broadcast([P, TC, n])
                link(nc.vector.tensor_reduce(top[:, row], values, AX.X, ALU.max))
                link(nc.vector.tensor_tensor(hit[:, :, 0:n], values, wide(top[:, row], n), ALU.is_equal))
                link(nc.vector.tensor_tensor(hit[:, :, 0:n], hit[:, :, 0:n], idx, ALU.mult))
                link(nc.vector.tensor_reduce(top[:, 3], hit[:, :, 0:n], AX.X, ALU.min))
                link(nc.vector.tensor_tensor(mask, idx, wide(top[:, 3], n), ALU.is_equal))

            dve.wait_ge(snapped, AHEAD + 2 * NB)
            link(nc.vector.tensor_reduce(rms[:], ssq[:], AX.X, ALU.add))
            nc.vector.tensor_scalar(rms[:], rms[:], 1.0 / D, EPS, ALU.mult, ALU.add).then_inc(exp_asked, 1)
            dve.wait_ge(exp_ready, 1)
            link(nc.vector.reciprocal(rinv2[:], rms[:]))
            dve.wait_ge(logits_out, AHEAD + TURNS)
            for t in range(TC):
                last = nc.vector.scalar_tensor_tensor(out=logit[:, t], in0=logit_sum[:, t], scalar=rinv2[:, t:t + 1],
                                                      in1=bias[:], op0=ALU.mult, op1=ALU.add)
            link(last)
            of_group, of_expert = logit[:, :, 0:GROUPS], logit[:, :, GROUPS:LOGITS]
            first_max(of_group, GROUPS, 0, first_group[:])
            nc.vector.tensor_tensor(to_exp[:, :, 0:GROUPS], of_group, wide(top[:, 0], GROUPS), ALU.subtract)
            link(nc.vector.tensor_scalar(first_group[:], first_group[:], FAR, -FAR, ALU.mult, ALU.add))
            link(nc.vector.tensor_tensor(masked[:].rearrange("p t (g e) -> p t g e", g=GROUPS),
                                         of_expert.rearrange("p t (g e) -> p t g e", g=GROUPS),
                                         first_group[:].unsqueeze(3).to_broadcast([P, TC, GROUPS, PER_GROUP]), ALU.add))
            first_max(masked[:], EXPERTS, 1, best[:])
            link(nc.vector.scalar_tensor_tensor(out=masked2[:], in0=best[:], scalar=-2.0 * FAR, in1=masked[:],
                                                op0=ALU.mult, op1=ALU.add))
            first_max(masked2[:], EXPERTS, 2, second[:])
            nc.vector.tensor_tensor(to_exp[:, :, GROUPS], top[:, 2], top[:, 1], ALU.subtract).then_inc(exp_asked, 1)
            nc.vector.tensor_tensor(sel[:], best[:], second[:], ALU.add).then_inc(sel_ready, 1)
            dve.wait_ge(exp_ready, 2)
            link(nc.vector.tensor_reduce(share[:, 0], exps[:, :, 0:GROUPS], AX.X, ALU.add))
            link(nc.vector.tensor_scalar(share[:, 1], exps[:, :, GROUPS], 1.0, None, ALU.add))
            link(nc.vector.tensor_tensor(share[:, 0], share[:, 0], share[:, 1], ALU.mult))
            link(nc.vector.reciprocal(share[:, 2], share[:, 0]))
            link(nc.vector.tensor_tensor(share[:, 3], share[:, 2], exps[:, :, GROUPS], ALU.mult))
            link(nc.vector.tensor_tensor(best[:], best[:], wide(share[:, 2], EXPERTS), ALU.mult))
            link(nc.vector.tensor_tensor(second[:], second[:], wide(share[:, 3], EXPERTS), ALU.mult))
            link(nc.vector.tensor_tensor(comb[:], best[:], second[:], ALU.add))
            dve.wait_ge(ranks_done, 1)
            link(nc.vector.tensor_reduce(fullest[:], bank[6][:, 2 * EXPERTS:3 * EXPERTS], AX.X, ALU.max))
            link(nc.vector.tensor_scalar(over[:, 0:MAX_ROUNDS - 1], bound, fullest[:, 0:1], None, ALU.is_lt))
            link(nc.vector.tensor_reduce(over[:, MAX_ROUNDS - 1:MAX_ROUNDS], over[:, 0:MAX_ROUNDS - 1], AX.X, ALU.add))
            link(nc.vector.tensor_tensor(rank[:].rearrange("p t e -> p (t e)"), bank[6][:, 0:2 * EXPERTS],
                                         sel[:].rearrange("p t e -> p (t e)"), ALU.mult))
            link(nc.vector.tensor_scalar(rank[:], rank[:], -1.0, None, ALU.add))
            nc.vector.tensor_scalar(rounds[:], over[:, MAX_ROUNDS - 1:MAX_ROUNDS], 1.0, None, ALU.add).then_inc(rounds_ready, 1)

            dve.wait_ge(rounds_ready, 1)
            more = dve.value_load(rounds[0:1, 0:1], min_val=1, max_val=MAX_ROUNDS)

            def add_block(j, turn, first):
                t, n = divmod(j, NB)
                use = first + j
                dve.wait_ge(swap_full, turn * SWAPS + use + 1)
                cols = xs[:, t, n * BLK:(n + 1) * BLK]
                nc.vector.tensor_tensor(cols, bank[6 + use % 2][:, :], cols, ALU.add).then_inc(swap_free[use % 2], 1)

            def pair(q, r, turn):
                dve.wait_ge(rank_moved, AHEAD + r)
                nc.vector.tensor_copy(pair_rank[:], rank[:, :, bass.ds(q * 2, 2)])
                nc.vector.tensor_copy(pair_comb[:], comb[:, :, bass.ds(q * 2, 2)]).then_inc(pair_cols, 1)
                dve.wait_ge(pair_cols, turn + 1)
                for t in range(TC):
                    for e in range(2):
                        for m, factor in ((pick, rinv2[:, t:t + 1]), (put, pair_comb[:, t, e:e + 1])):
                            last = nc.vector.tensor_scalar(m[:, t, e * CAP:(e + 1) * CAP], iota, pair_rank[:, t, e:e + 1],
                                                           factor, ALU.is_equal, ALU.mult)
                last.then_inc(pick_ready, 1)
                for g in (0, 2):
                    dve.wait_ge(swap_full, turn * SWAPS + g + 1)
                    nc.vector.tensor_tensor(picked[:, g * KPB:(g + 1) * KPB],
                                            bank[6][:, :].rearrange("p (k c) -> p k c", k=KPB),
                                            gffn[:, g * KPB:(g + 1) * KPB].unsqueeze(2).to_broadcast([P, KPB, 2 * CAP]),
                                            ALU.mult).then_inc(swap_free[0], 1)
                dve.wait_ge(silu_ready, turn + 1)
                nc.vector.tensor_tensor(act_rows[:], bank[1][:, :], silu[:], ALU.mult).then_inc(act_ready, 1)
                for i in range(2):
                    dve.wait_ge(swap_free[i], AHEAD + turn * (SWAPS // 2))
                for j in range(TC * NB):
                    add_block(j, turn, 4)
                dve.wait_ge(swap_full, turn * SWAPS + 13)
                nc.vector.tensor_copy(put_t[:], bank[6][:, 0:SEQ]).then_inc(swap_free[0], 1)

            with dve.Fori(0, more) as r:
                with dve.Fori(0, PAIRS) as q:
                    pair(q, r, r * PAIRS + q)
                nc.vector.tensor_scalar(rank[:], rank[:], -float(CAP), None, ALU.add).then_inc(rank_moved, 1)
            done = more * PAIRS
            for i in range(2):
                dve.wait_ge(swap_free[i], AHEAD + done * (SWAPS // 2))
            for j in range(TC * NB):
                add_block(j, done, 0)

            dve.wait_ge(gfin_in, 16)
            for t in range(TC):
                dve.wait_ge(last_squares, t + 1)
                nc.vector.tensor_scalar(rms[:, t:t + 1], ssq[:, t, 0:1], 1.0 / D, EPS, ALU.mult, ALU.add).then_inc(last_mean, 1)
                dve.wait_ge(last_root, t + 1)
                nc.vector.reciprocal(rinv[:, t:t + 1], rms[:, t:t + 1]).then_inc(last_rinv, 1)
                dve.wait_ge(last_rinv, t + 1)
                for half in range(2):
                    cols = slice(half * D // 2, (half + 1) * D // 2)
                    nc.vector.scalar_tensor_tensor(out=xs[:, t, cols], in0=xs[:, t, cols], scalar=rinv[:, t:t + 1],
                                                   in1=gfin[:, cols], op0=ALU.mult, op1=ALU.mult).then_inc(y_ready, 1)


def tables():
    consts = np.zeros((P, C_WIDTH), np.float32)
    consts[:, C_ID:C_ID + P] = np.eye(P)
    consts[:, C_TRI:C_TRI + P] = np.triu(np.ones((P, P)))
    consts[:, C_ONES:C_ONES + P] = 1.0
    consts[:, C_IOTA:C_IOTA + CAP] = np.arange(CAP)
    consts[:, C_IDX:C_IDX + EXPERTS] = np.arange(EXPERTS) - EXPERTS
    consts[:, C_FULL:] = CAP * np.arange(1, MAX_ROUNDS)
    angle = 2.0 * np.pi / SEQ * (np.outer(np.arange(SEQ), np.arange(SEQ)) % SEQ)
    half = SEQ // 2
    dft_tokens = np.concatenate([np.cos(angle[:, :half + 1]), np.sin(angle[:, 1:half])], 1) / np.sqrt(SEQ)
    angle = 2.0 * np.pi / HD * (np.outer(np.arange(HD), np.arange(HD)) % HD)
    dft_channels = np.concatenate([np.cos(angle), np.sin(angle)], 0) / np.sqrt(HD)
    windows = []
    for k in WINDOWS:
        m = np.zeros((SEQ, SEQ))
        for t in range(SEQ):
            lo, hi = max(t - (k - 1) // 2, 0), min(t + k // 2 + 1, SEQ)
            m[lo:hi, t] = 1.0 / (hi - lo)
        windows.append(m - np.eye(SEQ))
    f = np.float32
    return {"consts": consts, "dft_tokens": dft_tokens.astype(f), "dft_channels": dft_channels.astype(f),
            "pool_windows": np.concatenate(windows, 0).astype(f)}


_INS = ["x", "g_mix", "w_in", "w_pool", "pool_scale", "w_fourier", "w_out", "g_ffn", "w_group_router",
        "b_group_router", "w_expert_router", "b_expert_router", "w_gate", "w_up", "w_down", "g_final"]


def kernel(**inputs):
    import concourse.bacc as bacc
    from concourse.bass_utils import run_bass_kernel_spmd

    nc = bacc.Bacc("TRN2", target_bir_lowering=False, num_devices=1)
    arrays, args = {}, []
    given = {n: np.ascontiguousarray(inputs[n]) for n in _INS}
    given["x"] = given["x"].reshape(SEQ, D)
    given.update(tables())
    for name, a in given.items():
        arrays[f"in_{name}"] = a
        args.append(nc.dram_tensor(f"in_{name}", a.shape, mybir.dt.from_np(a.dtype), kind="ExternalInput").ap())
    args.append(nc.dram_tensor("out_y", (SEQ, D), mybir.dt.float32, kind="ExternalOutput").ap())
    build(nc, *args)
    r = run_bass_kernel_spmd(nc, [arrays], core_ids=[0])
    return r.results[0]["out_y"].reshape(1, SEQ, D)
```

```python
import concourse.bass as bass
from concourse import mybir
from concourse.alu_op_type import AluOpType as ALU
from contextlib import ExitStack
import numpy as np

P = 128
SEQ, D = 256, 2048
TC = SEQ // P
NB, BLK = 4, 512
KPB = BLK // P
KK = D // P
POOL_GROUPS, HEADS, HD = 4, 4, 256
HC = HD // P
WINDOWS = (2, 4, 8, 16)
GROUPS, PER_GROUP = 4, 4
EXPERTS = GROUPS * PER_GROUP
LOGITS = GROUPS + EXPERTS
FF = 512
FC = FF // P
CAP = 64
PAIRS = EXPERTS // 2
EPS = 1e-6
SLOTS = 16
MIX_SLOTS = 8
LATE_SLOTS = 4
SLOT = KPB * BLK
PAIR_SLABS = 2 * 3 * KPB
TURN_PAIRS = 2
TURNS = PAIRS // TURN_PAIRS
LAPS = TURN_PAIRS * PAIR_SLABS // SLOTS
HALF = SLOT // 2
FAR = 1.0e30

C_ID, C_TRI, C_ONES, C_IOTA, C_IDX = 0, P, 2 * P, 3 * P, 3 * P + CAP
C_FULL = C_IDX + EXPERTS
MAX_ROUNDS = SEQ // CAP
C_SUM = C_FULL + MAX_ROUNDS - 1
TILE = 32
C_WIDTH = C_SUM + LOGITS


def build(nc, x, g_mix, w_in, w_pool, pool_scale, w_fourier, w_out, g_ffn, w_group_router,
          b_group_router, w_expert_router, b_expert_router, w_gate, w_up, w_down, g_final,
          consts, dft_tokens, dft_channels, pool_windows, out):
    f32, f32r, i32 = mybir.dt.float32, mybir.dt.float32r, mybir.dt.int32
    ACT = mybir.ActivationFunctionType
    AX = mybir.AxisListType

    ctx = ExitStack()
    with ctx:
        def sem(name):
            return ctx.enter_context(nc.semaphore(name))

        def sb(name, shape, dt=f32, where=ctx):
            return where.enter_context(nc.sbuf_tensor(name, shape, dt))

        slot = [sb(f"slot{i}", [P, SLOT]) for i in range(SLOTS - LATE_SLOTS)]
        xs = sb("xs", [P, TC, D])
        u = sb("u", [P, TC, D])
        cst = sb("cst", [P, C_WIDTH])
        group_w = sb("group_w", [P, NB, KPB * GROUPS])
        expert_w = sb("expert_w", [P, NB, KPB * EXPERTS])
        router_w = sb("router_w", [P, KK, TILE])
        tiles = sb("tiles", [P, SEQ])
        gmix = sb("gmix", [P, KK])
        gffn = sb("gffn", [P, KK])
        pscale = sb("pscale", [P, POOL_GROUPS * HC])
        bias = sb("bias", [P, LOGITS])
        ssq = sb("ssq", [P, TC, NB])
        rms = sb("rms", [P, TC])
        rinv = sb("rinv", [P, TC])
        rinv2 = sb("rinv2", [P, TC])
        sel = sb("sel", [P, TC, EXPERTS])
        comb = sb("comb", [P, TC, EXPERTS])
        rank = sb("rank", [P, TC, EXPERTS])
        rounds = sb("rounds", [P, 1], i32)
        junk = sb("junk", [P, BLK])
        logit = sb("logit", [P, TC, LOGITS])
        hit = sb("hit", [P, TC, EXPERTS])
        other_group = sb("other_group", [P, TC, GROUPS])
        masked = sb("masked", [P, TC, EXPERTS])
        masked2 = sb("masked2", [P, TC, EXPERTS])
        best = sb("best", [P, TC, EXPERTS])
        second = sb("second", [P, TC, EXPERTS])
        top = sb("top", [P, 4, TC])
        to_exp = sb("to_exp", [P, TC, GROUPS + 1])
        exps = sb("exps", [P, TC, GROUPS + 1])
        share = sb("share", [P, 4, TC])
        over = sb("over", [P, MAX_ROUNDS])
        fullest = sb("fullest", [P, 1])
        pair_rank = sb("pair_rank", [P, TC, 2])
        pair_comb = sb("pair_comb", [P, TC, 2])

        early = ExitStack()
        tr_hi = sb("tr_hi", [P, KK, SEQ], f32r, early)
        tr_lo = sb("tr_lo", [P, KK, SEQ], f32r, early)
        w_hi = sb("w_hi", [P, 2, HALF], f32r, early)
        w_lo = sb("w_lo", [P, 2, HALF], f32r, early)
        mid = sb("mid", [P, 2, HEADS, HC * SEQ], f32, early)
        early.close()
        slot += [sb(f"slot{i}", [P, SLOT]) for i in range(SLOTS - LATE_SLOTS, SLOTS)]
        picked = sb("picked", [P, KK, 2 * CAP])
        expert_out = sb("expert_out", [2 * CAP, D])
        silu = sb("silu", [2 * CAP, FF])
        act_rows = sb("act_rows", [2 * CAP, FF])
        act_cols = sb("act_cols", [P, FC, 2 * CAP])
        pick = sb("pick", [P, TC, 2 * CAP])
        put = sb("put", [P, TC, 2 * CAP])
        put_t = sb("put_t", [2 * CAP, SEQ])
        gfin = sb("gfin", [P, D])

        bank = [ctx.enter_context(nc.psum_tensor(f"bank{i}", [P, BLK], f32)) for i in range(8)]

        ident, tri = cst[:, C_ID:C_ID + P], cst[:, C_TRI:C_TRI + P]
        tile_sum = cst[:, C_SUM:C_SUM + LOGITS]
        bound = cst[:, C_FULL:C_FULL + MAX_ROUNDS - 1]
        ones, iota = cst[:, C_ONES:C_ONES + P], cst[:, C_IOTA:C_IOTA + CAP]
        index = cst[:, C_IDX:C_IDX + EXPERTS]
        x2t = mid[:, 0].rearrange("p h n -> p (h n)").rearrange("p (b k n) -> p b k n", b=2, k=KPB)
        snap = u[:, :, :].rearrange("p t (k c) -> p t k c", k=KK)
        ab, pooled = mid[:, 0], mid[:, 1]
        pq = u[:, 0, :].rearrange("p (h n) -> p h n", h=HEADS)
        real = u[:, 1, :].rearrange("p (h n) -> p h n", h=HEADS)

        AHEAD = 1
        slot_full = [sem(f"slot_full{i}") for i in range(SLOTS)]
        slot_free = [sem(f"slot_free{i}") for i in range(SLOTS)]
        x_in = [sem(f"x_in{i}") for i in range(NB)]
        first_in = sem("first_in")
        small_in = sem("small_in")
        gfin_in = sem("gfin_in")
        x_turned = sem("x_turned")
        h_hi = sem("h_hi")
        h_lo = sem("h_lo")
        squares = sem("squares")
        mean_ready = sem("mean_ready")
        root_ready = sem("root_ready")
        rinv_ready = sem("rinv_ready")
        hi_ready = sem("hi_ready")
        lo_ready = sem("lo_ready")
        half_used = sem("half_used")
        u_out = sem("u_out")
        u_out_act = sem("u_out_act")
        unit_done = sem("unit_done")
        unit_act = sem("unit_act")
        unit_dve = sem("unit_dve")
        router_scaled = sem("router_scaled")
        x2_out = sem("x2_out")
        x2_turned = sem("x2_turned")
        x2t_out = sem("x2t_out")
        snapped = sem("snapped")
        x2_squares = sem("x2_squares")
        tiles_done = sem("tiles_done")
        tiles_out = sem("tiles_out")
        logits_done = sem("logits_done")
        step = sem("step")
        exp_ready = sem("exp_ready")
        exp_asked = sem("exp_asked")
        sel_ready = sem("sel_ready")
        ranks_done = sem("ranks_done")
        rounds_ready = sem("rounds_ready")
        zeroed = sem("zeroed")
        pair_cols = sem("pair_cols")
        pick_ready = sem("pick_ready")
        put_ready = sem("put_ready")
        rank_moved = sem("rank_moved")
        swap_full = sem("swap_full")
        swap_free = [sem(f"swap_free{i}") for i in range(2)]
        silu_ready = sem("silu_ready")
        act_ready = sem("act_ready")
        down_out = sem("down_out")
        scaled = sem("scaled")
        last_squares = sem("last_squares")
        last_mean = sem("last_mean")
        last_root = sem("last_root")
        last_rinv = sem("last_rinv")
        y_act = sem("y_act")
        y_dve = sem("y_dve")
        out_done = sem("out_done")

        w_in_v = w_in.rearrange("(g p k) (b n) -> b g p k n", p=P, k=KPB, b=NB)
        w_out_v = w_out.rearrange("(g k p) (b n) -> b g p k n", p=P, k=KPB, b=NB)
        gate_v = w_gate.rearrange("(q e) (g p k) n -> q e g p (k n)", e=2, p=P, k=KPB)
        up_v = w_up.rearrange("(q e) (g p k) n -> q e g p (k n)", e=2, p=P, k=KPB)
        down_v = w_down.rearrange("(q e) (c p) n -> q e c p n", e=2, p=P)

        HALVES = 2 * NB * NB
        U_AB, U_MEAN, U_PQ, U_WP, U_WF, UNITS = 0, 4, 8, 12, 16, 20
        SWAPS = 14
        GATHER_USE, SCATTER_USE = (0, 1, 2, 5), (3, 4, 6, 7, 8, 9, 10, 11)
        N_COS = SEQ // 2 + 1

        ORDER = [*range(MIX_SLOTS, SLOTS - LATE_SLOTS), *range(MIX_SLOTS), *range(SLOTS - LATE_SLOTS, SLOTS)]
        LOADED = [16 * 2 * NB * NB // MIX_SLOTS] * MIX_SLOTS + [32, 16, 16, 16] + [0] * LATE_SLOTS

        def slot_of(j):
            return ORDER[j % SLOTS]

        def freed(j, turn):
            return AHEAD + turn * LAPS + j // SLOTS + 1

        block = ctx.enter_context(nc.Block())

        @block.sync
        def _(sp):
            for ahead in slot_free:
                sp.sem_inc(ahead, AHEAD)
            def load_x(g):
                sp.dma_start(xs[:, :, g * BLK:(g + 1) * BLK],
                             x.rearrange("(t p) n -> p t n", p=P)[:, :, g * BLK:(g + 1) * BLK]).then_inc(x_in[g], 16)

            def load_slab(w, b, g, before):
                j = b * NB + g
                if before + j >= MIX_SLOTS:
                    sp.wait_ge(lo_ready, 2 * (before + j - MIX_SLOTS) + 2)
                s = j % MIX_SLOTS
                sp.dma_start(slot[s][:].rearrange("p (k n) -> p k n", k=KPB), w[b, g]).then_inc(slot_full[s], 16)

            load_x(0)
            for b in range(NB):
                for g in range(NB):
                    if b == 0 and g + 1 < NB:
                        load_x(g + 1)
                    load_slab(w_in_v, b, g, 0)
            for s, at, view in ((8, 0, dft_tokens.rearrange("(s p) n -> p s n", p=P)),
                                   (8, TC * SEQ, dft_channels.rearrange("(s p) n -> p s n", p=P)),
                                   (9, 0, pool_windows.rearrange("(s p) n -> p s n", p=P)),
                                   (10, 0, w_pool.rearrange("g (s p) n -> p (g s) n", p=P)),
                                   (11, 0, w_fourier.rearrange("g (s p) n -> p (g s) n", p=P))):
                n = view.shape[1] * view.shape[2]
                sp.dma_start(slot[s][:, at:at + n].rearrange("p (k n) -> p k n", k=view.shape[1]),
                             view).then_inc(slot_full[s], 16)
            for b in range(NB):
                for g in range(NB):
                    load_slab(w_out_v, b, g, NB * NB)
            sp.wait_ge(unit_done, UNITS)

            def load_turn(pairs, turn, first=False):
                for j in range(TURN_PAIRS * PAIR_SLABS):
                    i, k = divmod(j, PAIR_SLABS)
                    s = slot_of(j)
                    if k < 4 * NB:
                        e, w = k % 2, (gate_v, up_v)[k % 4 // 2]
                        src = w[bass.ds(pairs + i, 1), e, k // 4]
                    else:
                        src = down_v[bass.ds(pairs + i, 1), k % 2, (k - 4 * NB) // 2]
                    if first and j < SLOTS:
                        if s < MIX_SLOTS:
                            sp.wait_ge(lo_ready, 2 * HALVES - 2 * (MIX_SLOTS - 1 - s))
                        if s >= SLOTS - LATE_SLOTS:
                            sp.wait_ge(half_used, 2 * HALVES)
                    else:
                        sp.wait_ge(slot_free[s], freed(j, turn) - 1)
                    sp.dma_start(slot[s][:], src.rearrange("q p n -> p (q n)")).then_inc(slot_full[s], 16)

            load_turn(0, 0, first=True)
            with sp.Fori(1, TURNS) as q:
                load_turn(q * TURN_PAIRS, q)
            sp.wait_ge(rounds_ready, 1)
            more = sp.value_load(rounds[0:1, 0:1], min_val=1, max_val=MAX_ROUNDS)
            with sp.If(more > 1):
                with sp.Fori(1, more) as r:
                    with sp.Fori(0, TURNS) as q:
                        load_turn(q * TURN_PAIRS, r * TURNS + q)
            for ready, n, t, a, b in ((y_act, 1, 0, 0, D), (y_dve, 1, 1, D // 2, D), (y_act, 2, 1, 0, D // 2)):
                sp.wait_ge(ready, n)
                sp.dma_start(out[t * P:(t + 1) * P, a:b], u[:, t, a:b]).then_inc(out_done, 16)
            sp.wait_ge(out_done, 48)

        @block.tensor
        def _(pe):
            for ahead in swap_free:
                pe.sem_inc(ahead, AHEAD)
            pe.sem_inc(down_out, NB)
            pe.wait_ge(first_in, 16 * 2)

            def turn_x(g):
                pe.wait_ge(x_in[g], 16)
                if g >= 2:
                    pe.wait_ge(h_lo, KPB * (g - 1))
                for k in range(KPB):
                    for t in range(TC):
                        src = xs[:, t, g * BLK:(g + 1) * BLK].rearrange("p (c k) -> p k c", k=KPB)[:, k]
                        dst = bank[4 + (g % 2) * 2 + k // 2][:, (k % 2) * SEQ + t * P:(k % 2) * SEQ + (t + 1) * P]
                        last = nc.tensor.transpose(dst, src, ident)
                last.then_inc(x_turned, 1)

            def half_products(b, g, h, before):
                pe.wait_ge(lo_ready, before + (b * NB + g) * 2 + h + 1)
                for kl in range(2):
                    kk = g * KPB + h * 2 + kl
                    for t in range(TC):
                        dst = bank[2 * (b % 2) + t][:, :]
                        hi_t, lo_t = (m[:, kk, t * P:(t + 1) * P] for m in (tr_hi, tr_lo))
                        hi_w, lo_w = (m[:, h, kl * BLK:(kl + 1) * BLK] for m in (w_hi, w_lo))
                        nc.tensor.matmul(dst, hi_t, hi_w, start=kk == 0, stop=False)
                        nc.tensor.matmul(dst, hi_t, lo_w, start=False, stop=False)
                        last = nc.tensor.matmul(dst, lo_t, hi_w, start=False, stop=kk == KK - 1)
                last.then_inc(half_used, 1)

            turn_x(0)
            turn_x(1)
            for b in range(NB):
                if b >= 2:
                    pe.wait_ge(u_out, b - 1)
                    pe.wait_ge(u_out_act, b - 1)
                for g in range(NB):
                    if b == 0:
                        pe.wait_ge(h_lo, KPB * (g + 1))
                    half_products(b, g, 0, 0)
                    if b == 0 and g + 2 < NB:
                        turn_x(g + 2)
                    half_products(b, g, 1, 0)

            pe.wait_ge(u_out, NB)
            pe.wait_ge(u_out_act, NB)
            pe.wait_ge(small_in, 16 * 6)
            pe.wait_ge(slot_full[8], 32)
            for h in range(HEADS):
                for c in range(HC):
                    for s in range(TC):
                        col = D // 2 + h * HD + c * P
                        last = nc.tensor.matmul(bank[h][:, c * SEQ:(c + 1) * SEQ], u[:, s, col:col + P],
                                                slot[8][:, s * SEQ:(s + 1) * SEQ], start=s == 0, stop=s == TC - 1)
                last.then_inc(unit_done, 1)
            pe.wait_ge(slot_full[9], 16)
            for g in range(POOL_GROUPS):
                for c in range(HC):
                    for s in range(TC):
                        col = g * HD + c * P
                        last = nc.tensor.matmul(bank[4 + g][:, c * SEQ:(c + 1) * SEQ], u[:, s, col:col + P],
                                                slot[9][:, (g * TC + s) * SEQ:(g * TC + s + 1) * SEQ],
                                                start=s == 0, stop=s == TC - 1)
                last.then_inc(unit_done, 1)
            for h in range(HEADS):
                pe.wait_ge(unit_act, h + 1)
                for c in range(HC):
                    for part, (a, b) in enumerate(((0, N_COS), (N_COS, SEQ))):
                        for s in range(HC):
                            wcol = TC * SEQ + (part * HC + s) * HD + c * P
                            last = nc.tensor.matmul(bank[h][:, c * SEQ + a:c * SEQ + b], slot[8][:, wcol:wcol + P],
                                                    ab[:, h, s * SEQ + a:s * SEQ + b],
                                                    start=s == 0, stop=s == HC - 1)
                last.then_inc(unit_done, 1)
            pe.wait_ge(slot_full[10], 16)
            for g in range(POOL_GROUPS):
                pe.wait_ge(unit_dve, g + 1)
                for e in range(HC):
                    for c in range(HC):
                        wcol = (g * HC + c) * HD + e * P
                        last = nc.tensor.matmul(bank[4 + g][:, e * SEQ:(e + 1) * SEQ], slot[10][:, wcol:wcol + P],
                                                pooled[:, g, c * SEQ:(c + 1) * SEQ], start=c == 0, stop=c == HC - 1)
                last.then_inc(unit_done, 1)
            pe.wait_ge(slot_full[11], 16)
            for h in range(HEADS):
                pe.wait_ge(unit_dve, POOL_GROUPS + h + 1)
                for e in range(HC):
                    for c in range(HC):
                        wcol = (h * HC + c) * HD + e * P
                        last = nc.tensor.matmul(bank[h][:, e * SEQ:(e + 1) * SEQ], slot[11][:, wcol:wcol + P],
                                                real[:, h, c * SEQ:(c + 1) * SEQ], start=c == 0, stop=c == HC - 1)
                last.then_inc(unit_done, 1)

            def turn_x2(b):
                for t in range(TC):
                    pe.wait_ge(x2_out, TC * b + t + 1)
                    if b:
                        pe.wait_ge(x2t_out, TC * (b - 1) + t + 1)
                    for k in range(KPB):
                        src = xs[:, t, b * BLK:(b + 1) * BLK].rearrange("p (c k) -> p k c", k=KPB)[:, k]
                        last = nc.tensor.transpose(bank[4 + t][:, k * P:(k + 1) * P], src, ident)
                    last.then_inc(x2_turned, 1)

            def logit_products(b):
                pe.wait_ge(x2t_out, TC * (b + 1))
                for k in range(KPB):
                    last = nc.tensor.matmul(bank[6][k * TILE:(k + 1) * TILE, 0:SEQ], router_w[:, b * KPB + k],
                                            x2t[:, b % 2, k], start=b == 0, stop=b == NB - 1)
                if b == NB - 1:
                    last.then_inc(tiles_done, 1)

            pe.wait_ge(router_scaled, 1)
            for b in range(NB):
                if b >= 2:
                    pe.wait_ge(x2_out, TC * (b - 1))
                for g in range(NB):
                    if b == 0:
                        pe.wait_ge(unit_dve, 2 * POOL_GROUPS + HEADS + (0, 0, HEADS // 2, HEADS)[g])
                    for h in range(2):
                        half_products(b, g, h, HALVES)
                    if b and g == 0:
                        turn_x2(b - 1)
                    if b and g == 1:
                        logit_products(b - 1)
            turn_x2(NB - 1)
            logit_products(NB - 1)
            pe.wait_ge(tiles_out, 1)
            for t in range(TC):
                last = nc.tensor.matmul(bank[7][:, t * LOGITS:(t + 1) * LOGITS], tiles[:, t * P:(t + 1) * P], tile_sum,
                                        start=True, stop=True)
            last.then_inc(logits_done, 1)

            pe.wait_ge(sel_ready, 1)
            for col, parts in ((0, ((tri, 0),)), (1, ((ones, 0), (tri, 1))), (2, ((ones, 0), (ones, 1)))):
                for i, (m, t) in enumerate(parts):
                    last = nc.tensor.matmul(bank[6][:, col * EXPERTS:(col + 1) * EXPERTS], m, sel[:, t],
                                            start=i == 0, stop=i == len(parts) - 1)
            last.then_inc(ranks_done, 1)

            pe.wait_ge(rounds_ready, 1)
            more = pe.value_load(rounds[0:1, 0:1], min_val=1, max_val=MAX_ROUNDS)
            pe.wait_ge(snapped, NB * TC)
            pe.wait_ge(zeroed, 2)

            def read_out(pair, use):
                pe.wait_ge(swap_free[use % 2], AHEAD + pair * (SWAPS // 2) + use // 2 + 1)

            def bank_free(pair, use):
                pe.wait_ge(swap_free[use % 2], AHEAD + pair * (SWAPS // 2) + use // 2)

            def scatter(pair, j, use):
                t, n = divmod(j, NB)
                bank_free(pair, use)
                nc.tensor.matmul(bank[6 + use % 2][:, :], put_t[:, t * P:(t + 1) * P],
                                 expert_out[:, n * BLK:(n + 1) * BLK], start=True, stop=True).then_inc(swap_full, 1)

            def gather(pair, g):
                use = GATHER_USE[g]
                bank_free(pair, use)
                for k in range(KPB):
                    for t in range(TC):
                        last = nc.tensor.matmul(bank[6 + use % 2][:, k * P:(k + 1) * P], snap[:, t, g * KPB + k],
                                                pick[:, t], start=t == 0, stop=t == TC - 1)
                last.then_inc(swap_full, 1)

            def slab_in(j, turn):
                pe.wait_ge(slot_full[slot_of(j)], turn * (16 * LAPS) + LOADED[slot_of(j)] + 16 * (j // SLOTS + 1))

            def gate_up(pair, g, first, turn):
                for j in range(4):
                    slab_in(first + 4 * g + j, turn)
                read_out(pair, GATHER_USE[g])
                for k in range(KPB):
                    kk = g * KPB + k
                    for j in range(4):
                        e, which = j % 2, j // 2
                        s = slot_of(first + 4 * g + j)
                        last = nc.tensor.matmul(bank[which][e * CAP:(e + 1) * CAP, :],
                                                picked[:, kk, e * CAP:(e + 1) * CAP],
                                                slot[s][:, k * BLK:(k + 1) * BLK], start=kk == 0, stop=kk == KK - 1)
                        if k == KPB - 1:
                            last.then_inc(slot_free[s], 1)

            def run_pair(pair, first, turn):
                pe.wait_ge(pick_ready, pair + 1)
                gather(pair, 0)
                gather(pair, 1)
                gate_up(pair, 0, first, turn)
                gather(pair, 2)
                pe.wait_ge(down_out, NB + pair * NB)
                for j in (0, 1):
                    scatter(pair, j, SCATTER_USE[j])
                gate_up(pair, 1, first, turn)
                gather(pair, 3)
                for j in (2, 3, 4):
                    scatter(pair, j, SCATTER_USE[j])
                gate_up(pair, 2, first, turn)
                for j in (5, 6, 7):
                    scatter(pair, j, SCATTER_USE[j])
                gate_up(pair, 3, first, turn)
                pe.wait_ge(put_ready, pair + 1)
                bank_free(pair, 12)
                for t in range(TC):
                    last = nc.tensor.transpose(bank[6][:, t * P:(t + 1) * P], put[:, t], ident)
                last.then_inc(swap_full, 1)
                pe.wait_ge(act_ready, pair + 1)
                bank_free(pair, 13)
                for c in range(FC):
                    last = nc.tensor.transpose(bank[7][:, c * P:(c + 1) * P], act_rows[:, c * P:(c + 1) * P], ident)
                last.then_inc(swap_full, 1)
                read_out(pair, 13)
                for c in range(FC):
                    for e in range(2):
                        slab_in(first + 4 * NB + 2 * c + e, turn)
                    for n in range(NB):
                        for e in range(2):
                            s = slot_of(first + 4 * NB + 2 * c + e)
                            last = nc.tensor.matmul(bank[2 + n][e * CAP:(e + 1) * CAP, :],
                                                    act_cols[:, c, e * CAP:(e + 1) * CAP],
                                                    slot[s][:, n * BLK:(n + 1) * BLK],
                                                    start=c == 0, stop=c == FC - 1)
                            if n == NB - 1:
                                last.then_inc(slot_free[s], 1)

            with pe.Fori(0, more) as r:
                with pe.Fori(0, TURNS) as q:
                    turn = r * TURNS + q
                    for i in range(TURN_PAIRS):
                        run_pair(turn * TURN_PAIRS + i, i * PAIR_SLABS, turn)
            done = more * PAIRS
            bank_free(done, 0)
            for j in range(TC * NB):
                pe.wait_ge(down_out, done * NB + j % NB + 1)
                scatter(done, j, j)

        @block.scalar
        def _(act):
            act.dma_start(cst[:], consts).then_inc(first_in, 16)
            for dst, g, done_in in ((gmix, g_mix, first_in), (gffn, g_ffn, small_in)):
                act.dma_start(dst[:].rearrange("p (g k) -> p g k", k=KPB),
                              g.rearrange("(g p k) -> p g k", p=P, k=KPB)).then_inc(done_in, 16)
            with nc.allow_non_contiguous_dma(reason="eight scalars of a partition"):
                act.dma_start(pscale[:], pool_scale.rearrange("(c p) -> p c", p=P)).then_inc(small_in, 16)
            for dst, w in ((group_w, w_group_router), (expert_w, w_expert_router)):
                act.dma_start(dst[:], w.rearrange("(g p k) n -> p g (k n)", p=P, k=KPB)).then_inc(small_in, 16)
            for first, n, b in ((0, GROUPS, b_group_router), (GROUPS, EXPERTS, b_expert_router)):
                act.dma_start(bias[:, first:first + n], b.unsqueeze(0).to_broadcast([P, n])).then_inc(small_in, 16)

            act.wait_ge(first_in, 16 * 2)

            def h_block(g):
                act.wait_ge(x_turned, g + 1)
                for k in range(KPB):
                    kk = g * KPB + k
                    src = bank[4 + (g % 2) * 2 + k // 2][:, (k % 2) * SEQ:(k % 2 + 1) * SEQ]
                    nc.scalar.mul(tr_hi[:, kk], src, gmix[:, kk:kk + 1]).then_inc(h_hi, 1)

            def high_part(b, g, h, before):
                j = b * NB + g
                if h == 0:
                    act.wait_ge(slot_full[j % MIX_SLOTS], 16 * ((before // 2 + j) // MIX_SLOTS + 1))
                if before + 2 * j + h >= 2:
                    act.wait_ge(half_used, before + 2 * j + h - 1)
                nc.scalar.copy(w_hi[:, h], slot[j % MIX_SLOTS][:, h * HALF:(h + 1) * HALF]).then_inc(hi_ready, 1)

            def u_block(b):
                act.wait_ge(rinv_ready, 1)
                act.wait_ge(half_used, 2 * NB * (b + 1))
                nc.scalar.mul(u[:, 0, b * BLK:(b + 1) * BLK], bank[2 * (b % 2)][:, :], rinv[:, 0:1]).then_inc(u_out_act, 1)

            for b in range(NB):
                for g in range(NB):
                    if b == 0:
                        h_block(g)
                    for h in range(2):
                        high_part(b, g, h, 0)
                    if b == 1 and g < TC:
                        nc.scalar.activation(mid[:, g].rearrange("p h n -> p (h n)"), xs[:, g], ACT.Square,
                                             accum_out=ssq[:, g, 0:1]).then_inc(squares, 1)
                    if b == 1 and g == TC:
                        act.wait_ge(mean_ready, 1)
                        nc.scalar.activation(rms[:], rms[:], ACT.Sqrt).then_inc(root_ready, 1)
                        u_block(0)
                    if b >= 2 and g == 0:
                        u_block(b - 1)
            u_block(NB - 1)

            for h in range(HEADS):
                act.wait_ge(unit_done, U_AB + h + 1)
                nc.scalar.copy(ab[:, h], bank[h][:, :]).then_inc(unit_act, 1)
            for h in range(HEADS):
                act.wait_ge(unit_done, U_PQ + h + 1)
                nc.scalar.copy(pq[:, h], bank[h][:, :]).then_inc(unit_act, 1)
            for g in range(POOL_GROUPS):
                act.wait_ge(unit_done, U_WP + g + 1)
                for e in range(HC):
                    m = g * HC + e
                    last = nc.scalar.mul(tr_hi[:, m], bank[4 + g][:, e * SEQ:(e + 1) * SEQ], pscale[:, m:m + 1])
                last.then_inc(unit_act, 1)
            for h in range(HEADS):
                act.wait_ge(unit_done, U_WF + h + 1)
                m = (POOL_GROUPS + h) * HC
                nc.scalar.copy(tr_hi[:, m:m + HC].rearrange("p c n -> p (c n)"), bank[h][:, :]).then_inc(unit_act, 1)

            def turned_block(b):
                for t in range(TC):
                    act.wait_ge(x2_turned, TC * b + t + 1)
                    nc.scalar.copy(x2t[:, b % 2, :, t * P:(t + 1) * P],
                                   bank[4 + t][:, :].rearrange("p (k c) -> p k c", k=KPB)).then_inc(x2t_out, 1)

            def square_block(b):
                for t in range(TC):
                    act.wait_ge(x2_out, TC * b + t + 1)
                    if b or t:
                        act.wait_ge(x2_squares, TC * b + t)
                    nc.scalar.activation(junk[:], xs[:, t, b * BLK:(b + 1) * BLK], ACT.Square,
                                         accum_out=ssq[:, t, b:b + 1]).then_inc(x2_squares, 1)
            for b in range(NB):
                for g in range(NB):
                    for h in range(2):
                        high_part(b, g, h, HALVES)
                    if b and g == 1:
                        turned_block(b - 1)
                    if b and g == 2:
                        square_block(b - 1)
            square_block(NB - 1)
            turned_block(NB - 1)

            act.wait_ge(exp_asked, 1)
            nc.scalar.activation(rms[:], rms[:], ACT.Sqrt).then_inc(exp_ready, 1)

            act.wait_ge(logits_done, 1)
            act.dma_start(gfin[:], g_final.unsqueeze(0).to_broadcast([P, D])).then_inc(gfin_in, 16)
            act.wait_ge(exp_asked, 2)
            nc.scalar.activation(exps[:], to_exp[:], ACT.Exp).then_inc(exp_ready, 1)

            act.wait_ge(rounds_ready, 1)
            more = act.value_load(rounds[0:1, 0:1], min_val=1, max_val=MAX_ROUNDS)

            def run_pair(pair, first, turn):
                for g in (1, 2, 3):
                    use = GATHER_USE[g]
                    act.wait_ge(swap_full, pair * SWAPS + use + 1)
                    for k in range(KPB):
                        kk = g * KPB + k
                        last = nc.scalar.mul(picked[:, kk], bank[6 + use % 2][:, k * P:(k + 1) * P], gffn[:, kk:kk + 1])
                    last.then_inc(swap_free[use % 2], 1)
                end = first + 4 * NB - 1
                act.wait_ge(slot_free[slot_of(end)], freed(end, turn))
                nc.scalar.activation(silu[:], bank[0][:, :], ACT.Silu).then_inc(silu_ready, 1)
                act.wait_ge(swap_full, pair * SWAPS + SWAPS)
                nc.scalar.copy(act_cols[:].rearrange("p c n -> p (c n)"), bank[7][:, :]).then_inc(swap_free[1], 1)
                end = first + PAIR_SLABS - 1
                act.wait_ge(slot_free[slot_of(end)], freed(end, turn))
                for n in range(NB):
                    nc.scalar.copy(expert_out[:, n * BLK:(n + 1) * BLK], bank[2 + n][:, :]).then_inc(down_out, 1)

            with act.Fori(0, more) as r:
                with act.Fori(0, TURNS) as q:
                    turn = r * TURNS + q
                    for i in range(TURN_PAIRS):
                        run_pair(turn * TURN_PAIRS + i, i * PAIR_SLABS, turn)

            done = more * PAIRS
            for j in range(TC * NB):
                t, n = divmod(j, NB)
                act.wait_ge(swap_free[j % 2], AHEAD + done * (SWAPS // 2) + j // 2 + 1)
                if j:
                    act.wait_ge(last_squares, j)
                nc.scalar.activation(junk[:], xs[:, t, n * BLK:(n + 1) * BLK], ACT.Square,
                                     accum_out=ssq[:, t, n:n + 1]).then_inc(last_squares, 1)
                if j == NB + 1 or j == TC * NB - 1:
                    t = j // NB if j > NB + 1 else 0
                    act.wait_ge(last_mean, t + 1)
                    nc.scalar.activation(rms[:, t:t + 1], rms[:, t:t + 1], ACT.Sqrt).then_inc(last_root, 1)
                    act.wait_ge(last_rinv, t + 1)
                    act.wait_ge(scaled, NB + t * 2)
                    cols = slice(0, D // (t + 1))
                    nc.scalar.mul(u[:, t, cols], u[:, t, cols], rinv[:, t:t + 1]).then_inc(y_act, 1)

        @block.gpsimd
        def _(pool):
            pool.wait_ge(logits_done, 1)
            nc.gpsimd.memset(expert_out[:], 0.0).then_inc(zeroed, 1)
            nc.gpsimd.memset(put_t[:], 0.0).then_inc(zeroed, 1)
            pool.wait_ge(rounds_ready, 1)
            more = pool.value_load(rounds[0:1, 0:1], min_val=1, max_val=MAX_ROUNDS)
            pool.wait_ge(gfin_in, 16)
            for j in range(NB + 2):
                t, n = divmod(j, NB)
                pool.wait_ge(swap_free[j % 2], AHEAD + more * PAIRS * (SWAPS // 2) + j // 2 + 1)
                cols = slice(n * BLK, (n + 1) * BLK)
                nc.gpsimd.tensor_tensor(u[:, t, cols], xs[:, t, cols], gfin[:, cols], ALU.mult).then_inc(scaled, 1)

        @block.vector
        def _(dve):
            dve.sem_inc(rank_moved, AHEAD)
            steps = [0]

            def link(instruction):
                steps[0] += 1
                instruction.then_inc(step, 1)
                dve.wait_ge(step, steps[0])

            def h_block(g):
                for k in range(KPB):
                    kk = g * KPB + k
                    dve.wait_ge(h_hi, (kk // 2 + 1) * 2)
                    src = bank[4 + (g % 2) * 2 + k // 2][:, (k % 2) * SEQ:(k % 2 + 1) * SEQ]
                    nc.vector.scalar_tensor_tensor(out=tr_lo[:, kk], in0=src, scalar=gmix[:, kk:kk + 1],
                                                   in1=tr_hi[:, kk].bitcast(f32), op0=ALU.mult,
                                                   op1=ALU.subtract).then_inc(h_lo, 1)

            def low_part(b, g, h, before):
                j = b * NB + g
                dve.wait_ge(hi_ready, before + 2 * j + h + 1)
                nc.vector.tensor_tensor(w_lo[:, h], slot[j % MIX_SLOTS][:, h * HALF:(h + 1) * HALF],
                                        w_hi[:, h].bitcast(f32), ALU.subtract).then_inc(lo_ready, 1)

            def u_block(b):
                dve.wait_ge(half_used, 2 * NB * (b + 1))
                nc.vector.tensor_scalar(u[:, 1, b * BLK:(b + 1) * BLK], bank[2 * (b % 2) + 1][:, :],
                                        rinv[:, 1:2], None, ALU.mult).then_inc(u_out, 1)

            dve.wait_ge(first_in, 16 * 2)
            for b in range(NB):
                for g in range(NB):
                    if b == 0:
                        h_block(g)
                    for h in range(2):
                        low_part(b, g, h, 0)
                    if b == 1 and g == TC - 1:
                        dve.wait_ge(squares, TC)
                        nc.vector.tensor_scalar(rms[:], ssq[:, :, 0], 1.0 / D, EPS, ALU.mult, ALU.add).then_inc(mean_ready, 1)
                    if b == 1 and g == TC:
                        dve.wait_ge(root_ready, 1)
                        nc.vector.reciprocal(rinv[:], rms[:]).then_inc(rinv_ready, 1)
                        dve.wait_ge(rinv_ready, 1)
                        u_block(0)
                    if b >= 2 and g == 0:
                        u_block(b - 1)
            u_block(NB - 1)
            dve.wait_ge(small_in, 16 * 6)
            nc.vector.memset(router_w[:, :, LOGITS:TILE], 0.0)
            for w, first, n in ((group_w, 0, GROUPS), (expert_w, GROUPS, EXPERTS)):
                last = nc.vector.tensor_tensor(router_w[:, :, first:first + n],
                                               w[:].rearrange("p g (k n) -> p (g k) n", n=n),
                                               gffn[:].unsqueeze(2).to_broadcast([P, KK, n]), ALU.mult)
            last.then_inc(router_scaled, 1)

            for g in range(POOL_GROUPS):
                dve.wait_ge(unit_done, U_MEAN + g + 1)
                nc.vector.tensor_copy(pooled[:, g], bank[4 + g][:, :]).then_inc(unit_dve, 1)
            for h in range(HEADS):
                dve.wait_ge(unit_act, HEADS + h + 1)
                both = pq[:, h].rearrange("p (c n) -> p c n", c=HC)
                to = real[:, h].rearrange("p (c n) -> p c n", c=HC)
                mid_k = SEQ // 2
                nc.vector.tensor_copy(to[:, :, 0:mid_k + 1:mid_k], both[:, :, 0:mid_k + 1:mid_k])
                nc.vector.tensor_tensor(to[:, :, 1:mid_k], both[:, :, 1:mid_k], both[:, :, N_COS:SEQ], ALU.subtract)
                nc.vector.tensor_tensor(to[:, :, SEQ - 1:mid_k:-1], both[:, :, 1:mid_k], both[:, :, N_COS:SEQ],
                                        ALU.add).then_inc(unit_dve, 1)
            for g in range(POOL_GROUPS):
                dve.wait_ge(unit_act, 2 * HEADS + g + 1)
                for e in range(HC):
                    m = g * HC + e
                    last = nc.vector.scalar_tensor_tensor(out=tr_lo[:, m], in0=bank[4 + g][:, e * SEQ:(e + 1) * SEQ],
                                                          scalar=pscale[:, m:m + 1], in1=tr_hi[:, m].bitcast(f32),
                                                          op0=ALU.mult, op1=ALU.subtract)
                last.then_inc(unit_dve, 1)
            for h in range(HEADS):
                dve.wait_ge(unit_act, 3 * HEADS + h + 1)
                m = (POOL_GROUPS + h) * HC
                nc.vector.tensor_tensor(tr_lo[:, m:m + HC].rearrange("p c n -> p (c n)"), bank[h][:, :],
                                        tr_hi[:, m:m + HC].rearrange("p c n -> p (c n)").bitcast(f32),
                                        ALU.subtract).then_inc(unit_dve, 1)

            def x2_block(b):
                dve.wait_ge(half_used, HALVES + 2 * NB * (b + 1))
                for t in range(TC):
                    cols = xs[:, t, b * BLK:(b + 1) * BLK]
                    nc.vector.tensor_tensor(cols, bank[2 * (b % 2) + t][:, :], cols, ALU.add).then_inc(x2_out, 1)

            def snap_block(b):
                for t in range(TC):
                    dve.wait_ge(x2_out, TC * b + t + 1)
                    nc.vector.tensor_copy(snap[:, t, b * KPB:(b + 1) * KPB],
                                          xs[:, t, b * BLK:(b + 1) * BLK].rearrange("p (c k) -> p k c", k=KPB)).then_inc(snapped, 1)
            for b in range(NB):
                for g in range(NB):
                    for h in range(2):
                        low_part(b, g, h, HALVES)
                    if b and g == 0:
                        x2_block(b - 1)
                    if b and g == 1:
                        snap_block(b - 1)
            x2_block(NB - 1)
            snap_block(NB - 1)

            def wide(row, n):
                return row.unsqueeze(2).to_broadcast([P, TC, n])

            def first_max(values, n, row, mask, op=ALU.is_equal):
                idx = index[:, EXPERTS - n:]
                link(nc.vector.tensor_reduce(top[:, row], values, AX.X, ALU.max))
                for t in range(TC):
                    last = nc.vector.scalar_tensor_tensor(out=hit[:, t, 0:n], in0=values[:, t], scalar=top[:, row, t:t + 1],
                                                          in1=idx, op0=ALU.is_equal, op1=ALU.mult)
                link(last)
                link(nc.vector.tensor_reduce(top[:, 3], hit[:, :, 0:n], AX.X, ALU.min))
                link(nc.vector.tensor_tensor(mask, idx.unsqueeze(1).to_broadcast([P, TC, n]), wide(top[:, 3], n), op))

            dve.wait_ge(x2_squares, TC * NB)
            link(nc.vector.tensor_reduce(rms[:], ssq[:], AX.X, ALU.add))
            nc.vector.tensor_scalar(rms[:], rms[:], 1.0 / D, EPS, ALU.mult, ALU.add).then_inc(exp_asked, 1)
            dve.wait_ge(exp_ready, 1)
            link(nc.vector.reciprocal(rinv2[:], rms[:]))
            dve.wait_ge(tiles_done, 1)
            nc.vector.tensor_copy(tiles[:], bank[6][:, 0:SEQ]).then_inc(tiles_out, 1)
            dve.wait_ge(logits_done, 1)
            for t in range(TC):
                last = nc.vector.scalar_tensor_tensor(out=logit[:, t], in0=bank[7][:, t * LOGITS:(t + 1) * LOGITS],
                                                      scalar=rinv2[:, t:t + 1], in1=bias[:], op0=ALU.mult, op1=ALU.add)
            link(last)
            of_group, of_expert = logit[:, :, 0:GROUPS], logit[:, :, GROUPS:LOGITS]
            first_max(of_group, GROUPS, 0, other_group[:], ALU.not_equal)
            nc.vector.tensor_tensor(to_exp[:, :, 0:GROUPS], of_group, wide(top[:, 0], GROUPS), ALU.subtract)
            for t in range(TC):
                last = nc.vector.scalar_tensor_tensor(
                    out=masked[:, t].rearrange("p (g e) -> p g e", g=GROUPS),
                    in0=other_group[:, t].unsqueeze(2).to_broadcast([P, GROUPS, PER_GROUP]), scalar=-FAR,
                    in1=of_expert[:, t].rearrange("p (g e) -> p g e", g=GROUPS), op0=ALU.mult, op1=ALU.add)
            link(last)
            first_max(masked[:], EXPERTS, 1, best[:])
            link(nc.vector.scalar_tensor_tensor(out=masked2[:], in0=best[:], scalar=-2.0 * FAR, in1=masked[:],
                                                op0=ALU.mult, op1=ALU.add))
            first_max(masked2[:], EXPERTS, 2, second[:])
            nc.vector.tensor_tensor(to_exp[:, :, GROUPS], top[:, 2], top[:, 1], ALU.subtract).then_inc(exp_asked, 1)
            nc.vector.tensor_tensor(sel[:], best[:], second[:], ALU.add).then_inc(sel_ready, 1)
            dve.wait_ge(exp_ready, 2)
            link(nc.vector.tensor_reduce(share[:, 0], exps[:, :, 0:GROUPS], AX.X, ALU.add))
            link(nc.vector.tensor_scalar(share[:, 1], exps[:, :, GROUPS], 1.0, None, ALU.add))
            link(nc.vector.tensor_tensor(share[:, 0], share[:, 0], share[:, 1], ALU.mult))
            link(nc.vector.reciprocal(share[:, 2], share[:, 0]))
            link(nc.vector.tensor_tensor(share[:, 3], share[:, 2], exps[:, :, GROUPS], ALU.mult))
            link(nc.vector.tensor_tensor(best[:], best[:], wide(share[:, 2], EXPERTS), ALU.mult))
            link(nc.vector.tensor_tensor(second[:], second[:], wide(share[:, 3], EXPERTS), ALU.mult))
            link(nc.vector.tensor_tensor(comb[:], best[:], second[:], ALU.add))
            dve.wait_ge(ranks_done, 1)
            link(nc.vector.tensor_reduce(fullest[:], bank[6][:, 2 * EXPERTS:3 * EXPERTS], AX.X, ALU.max))
            link(nc.vector.tensor_scalar(over[:, 0:MAX_ROUNDS - 1], bound, fullest[:, 0:1], None, ALU.is_lt))
            nc.vector.tensor_tensor(rank[:].rearrange("p t e -> p (t e)"), bank[6][:, 0:2 * EXPERTS],
                                    sel[:].rearrange("p t e -> p (t e)"), ALU.mult)
            link(nc.vector.tensor_reduce(over[:, MAX_ROUNDS - 1:MAX_ROUNDS], over[:, 0:MAX_ROUNDS - 1], AX.X, ALU.add))
            nc.vector.tensor_scalar(rounds[:], over[:, MAX_ROUNDS - 1:MAX_ROUNDS], 1.0, None, ALU.add).then_inc(rounds_ready, 1)

            dve.wait_ge(rounds_ready, 1)
            more = dve.value_load(rounds[0:1, 0:1], min_val=1, max_val=MAX_ROUNDS)

            def add_block(pair, j, use):
                t, n = divmod(j, NB)
                dve.wait_ge(swap_full, pair * SWAPS + use + 1)
                cols = xs[:, t, n * BLK:(n + 1) * BLK]
                nc.vector.tensor_tensor(cols, bank[6 + use % 2][:, :], cols, ALU.add).then_inc(swap_free[use % 2], 1)

            def x2_written(pair):
                for i in range(2):
                    dve.wait_ge(swap_free[i], AHEAD + pair * (SWAPS // 2))

            def run_pair(first, r, pair):
                dve.wait_ge(rank_moved, AHEAD + r)
                nc.vector.tensor_copy(pair_rank[:], rank[:, :, bass.ds(first, 2)])
                nc.vector.tensor_copy(pair_comb[:], comb[:, :, bass.ds(first, 2)]).then_inc(pair_cols, 1)
                dve.wait_ge(pair_cols, pair + 1)
                for m in (pick, put):
                    for t in range(TC):
                        for e in range(2):
                            factor = rinv2[:, t:t + 1] if m is pick else pair_comb[:, t, e:e + 1]
                            last = nc.vector.tensor_scalar(m[:, t, e * CAP:(e + 1) * CAP], iota, pair_rank[:, t, e:e + 1],
                                                           factor, ALU.is_equal, ALU.mult)
                    if m is pick:
                        last.then_inc(pick_ready, 1)
                last.then_inc(put_ready, 1)
                dve.wait_ge(swap_full, pair * SWAPS + 1)
                nc.vector.tensor_tensor(picked[:, 0:KPB], bank[6][:, :].rearrange("p (k c) -> p k c", k=KPB),
                                        gffn[:, 0:KPB].unsqueeze(2).to_broadcast([P, KPB, 2 * CAP]),
                                        ALU.mult).then_inc(swap_free[0], 1)
                x2_written(pair)
                for j in range(TC * NB):
                    add_block(pair, j, SCATTER_USE[j])
                dve.wait_ge(silu_ready, pair + 1)
                nc.vector.tensor_tensor(act_rows[:], bank[1][:, :], silu[:], ALU.mult).then_inc(act_ready, 1)
                dve.wait_ge(swap_full, pair * SWAPS + 13)
                nc.vector.tensor_copy(put_t[:], bank[6][:, 0:SEQ]).then_inc(swap_free[0], 1)

            with dve.Fori(0, more) as r:
                with dve.Fori(0, TURNS) as q:
                    for i in range(TURN_PAIRS):
                        run_pair((q * TURN_PAIRS + i) * 2, r, (r * TURNS + q) * TURN_PAIRS + i)
                nc.vector.tensor_scalar(rank[:], rank[:], -float(CAP), None, ALU.add).then_inc(rank_moved, 1)
            done = more * PAIRS
            x2_written(done)

            def norm(t, part):
                if part == 0:
                    dve.wait_ge(last_squares, NB * (t + 1))
                    link(nc.vector.tensor_reduce(rms[:, t:t + 1], ssq[:, t], AX.X, ALU.add))
                    nc.vector.tensor_scalar(rms[:, t:t + 1], rms[:, t:t + 1], 1.0 / D, EPS, ALU.mult, ALU.add).then_inc(last_mean, 1)
                else:
                    dve.wait_ge(last_root, t + 1)
                    nc.vector.reciprocal(rinv[:, t:t + 1], rms[:, t:t + 1]).then_inc(last_rinv, 1)
            for j in range(TC * NB):
                add_block(done, j, j)
                if j == NB:
                    norm(0, 0)
                if j == NB + 1:
                    norm(0, 1)
            norm(1, 0)
            norm(1, 1)
            dve.wait_ge(last_rinv, TC)
            dve.wait_ge(gfin_in, 16)
            nc.vector.scalar_tensor_tensor(out=u[:, 1, D // 2:], in0=xs[:, 1, D // 2:], scalar=rinv[:, 1:2],
                                           in1=gfin[:, D // 2:], op0=ALU.mult, op1=ALU.mult).then_inc(y_dve, 1)


def tables():
    consts = np.zeros((P, C_WIDTH), np.float32)
    consts[:, C_ID:C_ID + P] = np.eye(P)
    consts[:, C_TRI:C_TRI + P] = np.triu(np.ones((P, P)))
    consts[:, C_ONES:C_ONES + P] = 1.0
    consts[:, C_IOTA:C_IOTA + CAP] = np.arange(1, CAP + 1)
    consts[:, C_IDX:C_IDX + EXPERTS] = np.arange(EXPERTS) - EXPERTS
    consts[:, C_FULL:C_FULL + MAX_ROUNDS - 1] = CAP * np.arange(1, MAX_ROUNDS)
    for k in range(P // TILE):
        consts[k * TILE:k * TILE + LOGITS, C_SUM:] = np.eye(LOGITS)
    angle = 2.0 * np.pi / SEQ * (np.outer(np.arange(SEQ), np.arange(SEQ)) % SEQ)
    half = SEQ // 2
    dft_tokens = np.concatenate([np.cos(angle[:, :half + 1]), np.sin(angle[:, 1:half])], 1) / np.sqrt(SEQ)
    angle = 2.0 * np.pi / HD * (np.outer(np.arange(HD), np.arange(HD)) % HD)
    dft_channels = np.concatenate([np.cos(angle), np.sin(angle)], 0) / np.sqrt(HD)
    windows = []
    for k in WINDOWS:
        m = np.zeros((SEQ, SEQ))
        for t in range(SEQ):
            lo, hi = max(t - (k - 1) // 2, 0), min(t + k // 2 + 1, SEQ)
            m[lo:hi, t] = 1.0 / (hi - lo)
        windows.append(m - np.eye(SEQ))
    f = np.float32
    return {"consts": consts, "dft_tokens": dft_tokens.astype(f), "dft_channels": dft_channels.astype(f),
            "pool_windows": np.concatenate(windows, 0).astype(f)}


_INS = ["x", "g_mix", "w_in", "w_pool", "pool_scale", "w_fourier", "w_out", "g_ffn", "w_group_router",
        "b_group_router", "w_expert_router", "b_expert_router", "w_gate", "w_up", "w_down", "g_final"]


def kernel(**inputs):
    import concourse.bacc as bacc
    from concourse.bass_utils import run_bass_kernel_spmd

    nc = bacc.Bacc("TRN2", target_bir_lowering=False, num_devices=1)
    arrays, args = {}, []
    given = {n: np.ascontiguousarray(inputs[n]) for n in _INS}
    given["x"] = given["x"].reshape(SEQ, D)
    given.update(tables())
    for name, a in given.items():
        arrays[f"in_{name}"] = a
        args.append(nc.dram_tensor(f"in_{name}", a.shape, mybir.dt.from_np(a.dtype), kind="ExternalInput").ap())
    args.append(nc.dram_tensor("out_y", (SEQ, D), mybir.dt.float32, kind="ExternalOutput").ap())
    build(nc, *args)
    r = run_bass_kernel_spmd(nc, [arrays], core_ids=[0])
    return r.results[0]["out_y"].reshape(1, SEQ, D)
```

```python
import concourse.bass as bass
from concourse import mybir
from concourse.alu_op_type import AluOpType as ALU
from contextlib import ExitStack
import numpy as np

P = 128
SEQ, D = 256, 2048
TC = SEQ // P
NB, BLK = 4, 512
KPB = BLK // P
KK = D // P
POOL_GROUPS, HEADS, HD = 4, 4, 256
HC = HD // P
WINDOWS = (2, 4, 8, 16)
GROUPS, PER_GROUP = 4, 4
EXPERTS = GROUPS * PER_GROUP
LOGITS = GROUPS + EXPERTS
FF = 512
FC = FF // P
CAP = 64
PAIRS = EXPERTS // 2
EPS = 1e-6
SLOTS = 16
MIX_SLOTS = 8
LATE_SLOTS = 4
SLOT = KPB * BLK
PAIR_SLABS = 2 * 3 * KPB
TURN_PAIRS = 2
TURNS = PAIRS // TURN_PAIRS
LAPS = TURN_PAIRS * PAIR_SLABS // SLOTS
HALF = SLOT // 2
WARM = (2, 2, 4, 2)
FAR = 1.0e30

C_ID, C_TRI, C_ONES, C_IOTA, C_IDX = 0, P, 2 * P, 3 * P, 3 * P + CAP
C_FULL = C_IDX + EXPERTS
MAX_ROUNDS = SEQ // CAP
C_SUM = C_FULL + MAX_ROUNDS - 1
TILE = 32
C_WIDTH = C_SUM + LOGITS


def build(nc, x, g_mix, w_in, w_pool, pool_scale, w_fourier, w_out, g_ffn, w_group_router,
          b_group_router, w_expert_router, b_expert_router, w_gate, w_up, w_down, g_final,
          consts, dft_tokens, dft_channels, pool_windows, out):
    f32, f32r, i32 = mybir.dt.float32, mybir.dt.float32r, mybir.dt.int32
    ACT = mybir.ActivationFunctionType
    AX = mybir.AxisListType

    ctx = ExitStack()
    with ctx:
        def sem(name):
            return ctx.enter_context(nc.semaphore(name))

        def sb(name, shape, dt=f32, where=ctx):
            return where.enter_context(nc.sbuf_tensor(name, shape, dt))

        slot = [sb(f"slot{i}", [P, SLOT]) for i in range(SLOTS - LATE_SLOTS)]
        xs = sb("xs", [P, TC, D])
        u = sb("u", [P, TC, D])
        cst = sb("cst", [P, C_WIDTH])
        group_w = sb("group_w", [P, NB, KPB * GROUPS])
        expert_w = sb("expert_w", [P, NB, KPB * EXPERTS])
        router_w = sb("router_w", [P, KK, TILE])
        tiles = sb("tiles", [P, SEQ])
        gmix = sb("gmix", [P, KK])
        gffn = sb("gffn", [P, KK])
        pscale = sb("pscale", [P, POOL_GROUPS * HC])
        bias = sb("bias", [P, LOGITS])
        ssq = sb("ssq", [P, TC, NB])
        rms = sb("rms", [P, TC])
        rinv = sb("rinv", [P, TC])
        rinv2 = sb("rinv2", [P, TC])
        sel = sb("sel", [P, TC, EXPERTS])
        comb = sb("comb", [P, TC, EXPERTS + 2])
        rank = sb("rank", [P, TC, EXPERTS + 2])
        rounds = sb("rounds", [P, 1], i32)
        junk = sb("junk", [P, BLK])
        logit = sb("logit", [P, TC, LOGITS])
        hit = sb("hit", [P, TC, EXPERTS])
        other_group = sb("other_group", [P, TC, GROUPS])
        masked = sb("masked", [P, TC, EXPERTS])
        masked2 = sb("masked2", [P, TC, EXPERTS])
        best = sb("best", [P, TC, EXPERTS])
        second = sb("second", [P, TC, EXPERTS])
        top = sb("top", [P, 4, TC])
        to_exp = sb("to_exp", [P, TC, GROUPS + 1])
        exps = sb("exps", [P, TC, GROUPS + 1])
        share = sb("share", [P, 4, TC])
        over = sb("over", [P, MAX_ROUNDS])
        fullest = sb("fullest", [P, 1])
        pair_rank = sb("pair_rank", [P, TC, 2])
        pair_comb = sb("pair_comb", [P, TC, 2])

        early = ExitStack()
        tr_hi = sb("tr_hi", [P, KK, SEQ], f32r, early)
        tr_lo = sb("tr_lo", [P, KK, SEQ], f32r, early)
        w_hi = sb("w_hi", [P, 2, HALF], f32r, early)
        w_lo = sb("w_lo", [P, 2, HALF], f32r, early)
        mid = sb("mid", [P, 2, HEADS, HC * SEQ], f32, early)
        early.close()
        slot += [sb(f"slot{i}", [P, SLOT]) for i in range(SLOTS - LATE_SLOTS, SLOTS)]
        picked = sb("picked", [P, KK, 2 * CAP])
        expert_out = sb("expert_out", [2 * CAP, D])
        silu = sb("silu", [2 * CAP, FF])
        act_rows = sb("act_rows", [2 * CAP, FF])
        act_cols = sb("act_cols", [P, FC, 2 * CAP])
        pick = sb("pick", [P, TC, 2 * CAP])
        put = sb("put", [P, TC, 2 * CAP])
        put_t = sb("put_t", [2 * CAP, SEQ])
        gfin = sb("gfin", [P, D])

        bank = [ctx.enter_context(nc.psum_tensor(f"bank{i}", [P, BLK], f32)) for i in range(8)]

        ident, tri = cst[:, C_ID:C_ID + P], cst[:, C_TRI:C_TRI + P]
        tile_sum = cst[:, C_SUM:C_SUM + LOGITS]
        bound = cst[:, C_FULL:C_FULL + MAX_ROUNDS - 1]
        ones, iota = cst[:, C_ONES:C_ONES + P], cst[:, C_IOTA:C_IOTA + CAP]
        index = cst[:, C_IDX:C_IDX + EXPERTS]
        x2t = mid[:, 0].rearrange("p h n -> p (h n)").rearrange("p (b k n) -> p b k n", b=2, k=KPB)
        snap = u[:, :, :].rearrange("p t (k c) -> p t k c", k=KK)
        block_squares, square_sum = u[:, 0, 2 * BLK:3 * BLK], u[:, :, 3 * BLK:]
        ab, pooled = mid[:, 0], mid[:, 1]
        pq = u[:, 0, :].rearrange("p (h n) -> p h n", h=HEADS)
        real = u[:, 1, :].rearrange("p (h n) -> p h n", h=HEADS)

        AHEAD = 1
        slot_full = [sem(f"slot_full{i}") for i in range(SLOTS)]
        slot_free = [sem(f"slot_free{i}") for i in range(SLOTS)]
        x_in = [sem(f"x_in{i}") for i in range(NB)]
        half_in = sem("half_in")
        first_in = sem("first_in")
        small_in = sem("small_in")
        gfin_in = sem("gfin_in")
        x_turned = sem("x_turned")
        h_hi = sem("h_hi")
        h_lo = sem("h_lo")
        squares = sem("squares")
        mean_ready = sem("mean_ready")
        root_ready = sem("root_ready")
        rinv_ready = sem("rinv_ready")
        hi_ready = sem("hi_ready")
        lo_ready = sem("lo_ready")
        half_used = sem("half_used")
        first_chunk = sem("first_chunk")
        u_out = sem("u_out")
        u_out_act = sem("u_out_act")
        unit_done = sem("unit_done")
        unit_act = sem("unit_act")
        unit_dve = sem("unit_dve")
        router_scaled = sem("router_scaled")
        x2_out = sem("x2_out")
        x2_turned = sem("x2_turned")
        x2t_out = sem("x2t_out")
        snapped = sem("snapped")
        x2_squares = sem("x2_squares")
        tiles_done = sem("tiles_done")
        tiles_out = sem("tiles_out")
        logits_done = sem("logits_done")
        step = sem("step")
        exp_ready = sem("exp_ready")
        exp_asked = sem("exp_asked")
        sel_ready = sem("sel_ready")
        ranks_done = sem("ranks_done")
        rounds_ready = sem("rounds_ready")
        pair_cols = sem("pair_cols")
        pick_ready = sem("pick_ready")
        put_ready = sem("put_ready")
        rank_moved = sem("rank_moved")
        swap_full = sem("swap_full")
        swap_free = [sem(f"swap_free{i}") for i in range(2)]
        silu_ready = sem("silu_ready")
        act_ready = sem("act_ready")
        down_out = sem("down_out")
        scaled = sem("scaled")
        pool_squares = sem("pool_squares")
        pool_block = sem("pool_block")
        last_squares = sem("last_squares")
        last_mean = sem("last_mean")
        last_root = sem("last_root")
        last_rinv = sem("last_rinv")
        y_act = sem("y_act")
        y_dve = sem("y_dve")
        out_done = sem("out_done")

        w_in_v = w_in.rearrange("(g p k) (b n) -> b g p k n", p=P, k=KPB, b=NB)
        w_out_v = w_out.rearrange("(g k p) (b n) -> b g p k n", p=P, k=KPB, b=NB)
        gate_v = w_gate.rearrange("(q e) (g p h k) n -> q g h p e (k n)", e=2, p=P, h=2, k=KPB // 2)
        up_v = w_up.rearrange("(q e) (g p h k) n -> q g h p e (k n)", e=2, p=P, h=2, k=KPB // 2)
        down_v = w_down.rearrange("(q e) (c p) (n m) -> q n c p e m", e=2, p=P, n=2)

        HALVES = 2 * NB * NB
        U_AB, U_MEAN, U_PQ, U_WP, U_WF, UNITS = 0, 4, 8, 12, 16, 20
        U_GATHER, U_PUT, U_ACT, U_SCATTER, SWAPS = 0, 4, 5, 6, 14
        N_COS = SEQ // 2 + 1

        ORDER = [*range(MIX_SLOTS, SLOTS - LATE_SLOTS), *range(MIX_SLOTS), *range(SLOTS - LATE_SLOTS, SLOTS)]
        LOADED = [16 * 2 * NB * NB // MIX_SLOTS] * MIX_SLOTS + [32, 16, 16, 16] + [0] * LATE_SLOTS

        def slot_of(j):
            return ORDER[j % SLOTS]

        def freed(j, turn):
            return AHEAD + turn * LAPS + j // SLOTS + 1

        def last_use(more, n):
            return more * (PAIRS * (SWAPS // 2)) + U_SCATTER // 2 + n + 1

        block = ctx.enter_context(nc.Block())

        @block.sync
        def _(sp):
            for ahead in slot_free:
                sp.sem_inc(ahead, AHEAD)
            def load_x(g):
                sp.dma_start(xs[:, :, g * BLK:(g + 1) * BLK],
                             x.rearrange("(t p) n -> p t n", p=P)[:, :, g * BLK:(g + 1) * BLK]).then_inc(x_in[g], 16)

            def load_slab(w, b, g, before):
                j = b * NB + g
                if before + j >= MIX_SLOTS:
                    sp.wait_ge(lo_ready, 2 * (before + j - MIX_SLOTS) + 2)
                s = j % MIX_SLOTS
                sp.dma_start(slot[s][:].rearrange("p (k n) -> p k n", k=KPB), w[b, g]).then_inc(slot_full[s], 16)

            def load_small():
                sp.dma_start(gffn[:].rearrange("p (g k) -> p g k", k=KPB),
                             g_ffn.rearrange("(g p k) -> p g k", p=P, k=KPB)).then_inc(small_in, 16)
                with nc.allow_non_contiguous_dma(reason="eight scalars of a partition"):
                    sp.dma_start(pscale[:], pool_scale.rearrange("(c p) -> p c", p=P)).then_inc(small_in, 16)
                for dst, w in ((group_w, w_group_router), (expert_w, w_expert_router)):
                    sp.dma_start(dst[:], w.rearrange("(g p k) n -> p g (k n)", p=P, k=KPB)).then_inc(small_in, 16)
                for first, n, b in ((0, GROUPS, b_group_router), (GROUPS, EXPERTS, b_expert_router)):
                    sp.dma_start(bias[:, first:first + n], b.unsqueeze(0).to_broadcast([P, n])).then_inc(small_in, 16)

            load_x(0)
            sp.dma_start(slot[0][:, 0:HALF].rearrange("p (k n) -> p k n", k=KPB // 2),
                         w_in_v[0, 0][:, 0:KPB // 2]).then_inc(half_in, 16)
            load_x(1)
            sp.dma_start(slot[0][:, HALF:].rearrange("p (k n) -> p k n", k=KPB // 2),
                         w_in_v[0, 0][:, KPB // 2:]).then_inc(slot_full[0], 16)
            for b in range(NB):
                for g in range(NB):
                    if b or g:
                        load_slab(w_in_v, b, g, 0)
                    if b == 0 and 1 <= g < NB - 1:
                        load_x(g + 1)
                if b == 0:
                    load_small()
            for s, at, view in ((8, 0, dft_tokens.rearrange("(s p) n -> p s n", p=P)),
                                   (8, TC * SEQ, dft_channels.rearrange("(s p) n -> p s n", p=P)),
                                   (9, 0, pool_windows.rearrange("(s p) n -> p s n", p=P)),
                                   (10, 0, w_pool.rearrange("g (s p) n -> p (g s) n", p=P)),
                                   (11, 0, w_fourier.rearrange("g (s p) n -> p (g s) n", p=P))):
                n = view.shape[1] * view.shape[2]
                sp.dma_start(slot[s][:, at:at + n].rearrange("p (k n) -> p k n", k=view.shape[1]),
                             view).then_inc(slot_full[s], 16)
            for b in range(NB):
                for g in range(NB):
                    load_slab(w_out_v, b, g, NB * NB)
            sp.wait_ge(unit_done, UNITS)

            def load_turn(pairs, turn, first=False):
                for j in range(TURN_PAIRS * PAIR_SLABS):
                    i, k = divmod(j, PAIR_SLABS)
                    s = slot_of(j)
                    if k < 4 * NB:
                        src = (gate_v, up_v)[k % 4 // 2][bass.ds(pairs + i, 1), k // 4, k % 2]
                    else:
                        src = down_v[bass.ds(pairs + i, 1), (k - 4 * NB) // FC, k % FC]
                    if first and j < SLOTS:
                        if s < MIX_SLOTS:
                            sp.wait_ge(lo_ready, 2 * HALVES - 2 * (MIX_SLOTS - 1 - s))
                        if s >= SLOTS - LATE_SLOTS:
                            sp.wait_ge(half_used, 2 * HALVES)
                    else:
                        sp.wait_ge(slot_free[s], freed(j, turn) - 1)
                    sp.dma_start(slot[s][:].rearrange("p (e m) -> p e m", e=2),
                                 src.rearrange("q p e m -> p (q e) m")).then_inc(slot_full[s], 16)

            load_turn(0, 0, first=True)
            with sp.Fori(1, TURNS) as q:
                load_turn(q * TURN_PAIRS, q)
            sp.wait_ge(rounds_ready, 1)
            more = sp.value_load(rounds[0:1, 0:1], min_val=1, max_val=MAX_ROUNDS)
            with sp.If(more > 1):
                with sp.Fori(1, more) as r:
                    with sp.Fori(0, TURNS) as q:
                        load_turn(q * TURN_PAIRS, r * TURNS + q)
            for t in range(TC):
                for ready, a, b in ((y_act, 0, D // 2), (y_dve, D // 2, D)):
                    sp.wait_ge(ready, t + 1)
                    sp.dma_start(out[t * P:(t + 1) * P, a:b], u[:, t, a:b]).then_inc(out_done, 16)
            sp.wait_ge(out_done, 16 * 2 * TC)

        @block.tensor
        def _(pe):
            for ahead in swap_free:
                pe.sem_inc(ahead, SWAPS // 2)
            pe.wait_ge(first_in, 16 * 2)

            def keep_warm(products):
                for _ in range(products):
                    nc.tensor.matmul(bank[0][:, 0:C_IOTA], ident, cst[:, 0:C_IOTA], start=True, stop=True)

            def turn_x(g):
                pe.wait_ge(x_in[g], 16)
                if g >= 2:
                    pe.wait_ge(h_lo, KPB * (g - 1))
                for k in range(KPB):
                    for t in range(TC):
                        src = xs[:, t, g * BLK:(g + 1) * BLK].rearrange("p (c k) -> p k c", k=KPB)[:, k]
                        dst = bank[4 + (g % 2) * 2 + k // 2][:, (k % 2) * SEQ + t * P:(k % 2) * SEQ + (t + 1) * P]
                        last = nc.tensor.transpose(dst, src, ident)
                last.then_inc(x_turned, 1)

            def half_products(b, g, h, before):
                pe.wait_ge(lo_ready, before + (b * NB + g) * 2 + h + 1)
                for t in range(TC):
                    dst = bank[2 * (b % 2) + t][:, :]
                    for kl in range(2):
                        kk = g * KPB + h * 2 + kl
                        hi_t, lo_t = (m[:, kk, t * P:(t + 1) * P] for m in (tr_hi, tr_lo))
                        hi_w, lo_w = (m[:, h, kl * BLK:(kl + 1) * BLK] for m in (w_hi, w_lo))
                        nc.tensor.matmul(dst, hi_t, hi_w, start=kk == 0, stop=False)
                        nc.tensor.matmul(dst, hi_t, lo_w, start=False, stop=False)
                        last = nc.tensor.matmul(dst, lo_t, hi_w, start=False, stop=kk == KK - 1)
                    if before and kk == KK - 1 and t == 0:
                        last.then_inc(first_chunk, 1)
                last.then_inc(half_used, 1)

            keep_warm(1)
            turn_x(0)
            keep_warm(WARM[0])
            for b in range(NB):
                if b >= 2:
                    pe.wait_ge(u_out, b - 1)
                    pe.wait_ge(u_out_act, b - 1)
                for g in range(NB):
                    for h in range(2):
                        if b == 0:
                            pe.wait_ge(h_lo, KPB * g + KPB // 2 * (h + 1))
                        half_products(b, g, h, 0)
                        if b == 0 and h == 0 and g + 1 < NB:
                            turn_x(g + 1)

            pe.wait_ge(slot_full[8], 32)
            for h in range(HEADS):
                if h % 2 == 0:
                    pe.wait_ge(u_out, NB - 1 + h // 2)
                    pe.wait_ge(u_out_act, NB - 1 + h // 2)
                for c in range(HC):
                    for s in range(TC):
                        col = D // 2 + h * HD + c * P
                        last = nc.tensor.matmul(bank[h][:, c * SEQ:(c + 1) * SEQ], u[:, s, col:col + P],
                                                slot[8][:, s * SEQ:(s + 1) * SEQ], start=s == 0, stop=s == TC - 1)
                last.then_inc(unit_done, 1)
            pe.wait_ge(slot_full[9], 16)
            for g in range(POOL_GROUPS):
                for c in range(HC):
                    for s in range(TC):
                        col = g * HD + c * P
                        last = nc.tensor.matmul(bank[4 + g][:, c * SEQ:(c + 1) * SEQ], u[:, s, col:col + P],
                                                slot[9][:, (g * TC + s) * SEQ:(g * TC + s + 1) * SEQ],
                                                start=s == 0, stop=s == TC - 1)
                last.then_inc(unit_done, 1)
            for h in range(HEADS):
                pe.wait_ge(unit_act, h + 1)
                for c in range(HC):
                    for part, (a, b) in enumerate(((0, N_COS), (N_COS, SEQ))):
                        for s in range(HC):
                            wcol = TC * SEQ + (part * HC + s) * HD + c * P
                            last = nc.tensor.matmul(bank[h][:, c * SEQ + a:c * SEQ + b], slot[8][:, wcol:wcol + P],
                                                    ab[:, h, s * SEQ + a:s * SEQ + b],
                                                    start=s == 0, stop=s == HC - 1)
                last.then_inc(unit_done, 1)
            pe.wait_ge(slot_full[10], 16)
            for g in range(POOL_GROUPS):
                pe.wait_ge(unit_dve, g + 1)
                for e in range(HC):
                    for c in range(HC):
                        wcol = (g * HC + c) * HD + e * P
                        last = nc.tensor.matmul(bank[4 + g][:, e * SEQ:(e + 1) * SEQ], slot[10][:, wcol:wcol + P],
                                                pooled[:, g, c * SEQ:(c + 1) * SEQ], start=c == 0, stop=c == HC - 1)
                last.then_inc(unit_done, 1)
            pe.wait_ge(slot_full[11], 16)
            for h in range(HEADS):
                pe.wait_ge(unit_dve, POOL_GROUPS + h + 1)
                for e in range(HC):
                    for c in range(HC):
                        wcol = (h * HC + c) * HD + e * P
                        last = nc.tensor.matmul(bank[h][:, e * SEQ:(e + 1) * SEQ], slot[11][:, wcol:wcol + P],
                                                real[:, h, c * SEQ:(c + 1) * SEQ], start=c == 0, stop=c == HC - 1)
                last.then_inc(unit_done, 1)

            def turn_x2(b):
                for t in range(TC):
                    pe.wait_ge(x2_out, TC * b + t + 1)
                    if b:
                        pe.wait_ge(x2t_out, TC * (b - 1) + t + 1)
                    for k in range(KPB):
                        src = xs[:, t, b * BLK:(b + 1) * BLK].rearrange("p (c k) -> p k c", k=KPB)[:, k]
                        last = nc.tensor.transpose(bank[4 + t][:, k * P:(k + 1) * P], src, ident)
                    last.then_inc(x2_turned, 1)

            def logit_products(b):
                pe.wait_ge(x2t_out, TC * (b + 1))
                for k in range(KPB):
                    last = nc.tensor.matmul(bank[6][k * TILE:(k + 1) * TILE, 0:SEQ], router_w[:, b * KPB + k],
                                            x2t[:, b % 2, k], start=b == 0, stop=b == NB - 1)
                if b == NB - 1:
                    last.then_inc(tiles_done, 1)

            pe.wait_ge(router_scaled, 1)
            for b in range(NB):
                if b >= 2:
                    pe.wait_ge(x2_out, TC * (b - 1))
                for g in range(NB):
                    if b == 0:
                        pe.wait_ge(unit_dve, 2 * POOL_GROUPS + HEADS + (HEADS // 2, HEADS // 2, HEADS // 2, HEADS)[g])
                    for h in range(2):
                        half_products(b, g, h, HALVES)
                    if b and g == 0:
                        turn_x2(b - 1)
                    if b and g == 1:
                        logit_products(b - 1)
            turn_x2(NB - 1)
            logit_products(NB - 1)
            keep_warm(WARM[1])
            pe.wait_ge(tiles_out, 1)
            for t in range(TC):
                last = nc.tensor.matmul(bank[7][:, t * LOGITS:(t + 1) * LOGITS], tiles[:, t * P:(t + 1) * P], tile_sum,
                                        start=True, stop=True)
            last.then_inc(logits_done, 1)
            keep_warm(WARM[2])

            pe.wait_ge(sel_ready, 1)
            for col, parts in ((0, ((tri, 0),)), (1, ((ones, 0), (tri, 1))), (2, ((ones, 0), (ones, 1)))):
                for i, (m, t) in enumerate(parts):
                    last = nc.tensor.matmul(bank[6][:, col * EXPERTS:(col + 1) * EXPERTS], m, sel[:, t],
                                            start=i == 0, stop=i == len(parts) - 1)
            last.then_inc(ranks_done, 1)
            keep_warm(WARM[3])

            pe.wait_ge(rounds_ready, 1)
            more = pe.value_load(rounds[0:1, 0:1], min_val=1, max_val=MAX_ROUNDS)
            pe.wait_ge(snapped, NB * TC)

            def read_out(pair, use):
                pe.wait_ge(swap_free[use % 2], pair * (SWAPS // 2) + SWAPS // 2 + use // 2 + 1)

            def bank_free(pair, use):
                pe.wait_ge(swap_free[use % 2], pair * (SWAPS // 2) + SWAPS // 2 + use // 2)

            def gather(pair, g):
                use = U_GATHER + g
                bank_free(pair, use)
                for k in range(KPB):
                    for t in range(TC):
                        last = nc.tensor.matmul(bank[6 + use % 2][:, k * P:(k + 1) * P], snap[:, t, g * KPB + k],
                                                pick[:, t], start=t == 0, stop=t == TC - 1)
                last.then_inc(swap_full, 1)

            def slab_in(j, turn):
                pe.wait_ge(slot_full[slot_of(j)], turn * (16 * LAPS) + LOADED[slot_of(j)] + 16 * (j // SLOTS + 1))

            def gate_up(pair, which, g, first, turn):
                read_out(pair, U_GATHER + g)
                for k in range(KPB):
                    s = slot_of(first + 4 * g + 2 * which + k // 2)
                    if k % 2 == 0:
                        slab_in(first + 4 * g + 2 * which + k // 2, turn)
                    kk = g * KPB + k
                    for e in range(2):
                        at = (e * 2 + k % 2) * BLK
                        last = nc.tensor.matmul(bank[which][e * CAP:(e + 1) * CAP, :],
                                                picked[:, kk, e * CAP:(e + 1) * CAP],
                                                slot[s][:, at:at + BLK], start=kk == 0, stop=kk == KK - 1)
                    if k % 2:
                        last.then_inc(slot_free[s], 1)

            def down(half, chunks, first, turn):
                for c in chunks:
                    s = slot_of(first + 4 * NB + half * FC + c)
                    slab_in(first + 4 * NB + half * FC + c, turn)
                    for n in range(2):
                        for e in range(2):
                            at = (e * 2 + n) * BLK
                            last = nc.tensor.matmul(bank[2 + 2 * half + n][e * CAP:(e + 1) * CAP, :],
                                                    act_cols[:, c, e * CAP:(e + 1) * CAP],
                                                    slot[s][:, at:at + BLK], start=c == 0, stop=c == FC - 1)
                    last.then_inc(slot_free[s], 1)

            def scatter(pair, n):
                pe.wait_ge(down_out, pair * NB + n + 1)
                for t in range(TC):
                    use = U_SCATTER + n * TC + t
                    bank_free(pair, use)
                    nc.tensor.matmul(bank[6 + use % 2][:, :], put_t[:, t * P:(t + 1) * P],
                                     expert_out[:, n * BLK:(n + 1) * BLK], start=True, stop=True).then_inc(swap_full, 1)

            def run_pair(pair, first, turn):
                pe.wait_ge(pick_ready, pair + 1)
                gather(pair, 0)
                gate_up(pair, 0, 0, first, turn)
                gather(pair, 1)
                gate_up(pair, 1, 0, first, turn)
                gather(pair, 2)
                gather(pair, 3)
                for g in (1, 2):
                    for which in range(2):
                        gate_up(pair, which, g, first, turn)
                pe.wait_ge(put_ready, pair + 1)
                bank_free(pair, U_PUT)
                for t in range(TC):
                    last = nc.tensor.transpose(bank[6][:, t * P:(t + 1) * P], put[:, t], ident)
                last.then_inc(swap_full, 1)
                for which in range(2):
                    gate_up(pair, which, 3, first, turn)
                pe.wait_ge(act_ready, pair + 1)
                bank_free(pair, U_ACT)
                for c in range(FC):
                    last = nc.tensor.transpose(bank[7][:, c * P:(c + 1) * P], act_rows[:, c * P:(c + 1) * P], ident)
                last.then_inc(swap_full, 1)
                read_out(pair, U_PUT)
                read_out(pair, U_ACT)
                down(0, range(FC), first, turn)
                down(1, (0,), first, turn)
                scatter(pair, 0)
                scatter(pair, 1)
                down(1, range(1, FC), first, turn)
                scatter(pair, 2)
                scatter(pair, 3)

            with pe.Fori(0, more) as r:
                with pe.Fori(0, TURNS) as q:
                    turn = r * TURNS + q
                    for i in range(TURN_PAIRS):
                        run_pair(turn * TURN_PAIRS + i, i * PAIR_SLABS, turn)

        @block.scalar
        def _(act):
            act.dma_start(cst[:], consts).then_inc(first_in, 16)
            act.dma_start(gmix[:].rearrange("p (g k) -> p g k", k=KPB),
                          g_mix.rearrange("(g p k) -> p g k", p=P, k=KPB)).then_inc(first_in, 16)

            act.wait_ge(first_in, 16 * 2)
            nc.scalar.copy(junk[:, 0:KK], gmix[:])

            def h_block(g):
                act.wait_ge(x_turned, g + 1)
                for k in range(KPB):
                    kk = g * KPB + k
                    src = bank[4 + (g % 2) * 2 + k // 2][:, (k % 2) * SEQ:(k % 2 + 1) * SEQ]
                    nc.scalar.mul(tr_hi[:, kk], src, gmix[:, kk:kk + 1]).then_inc(h_hi, 1)

            def high_part(b, g, h, before):
                j = b * NB + g
                first = before + j == 0
                if first and h == 0:
                    act.wait_ge(half_in, 16)
                elif first or h == 0:
                    act.wait_ge(slot_full[j % MIX_SLOTS], 16 * ((before // 2 + j) // MIX_SLOTS + 1))
                if before + 2 * j + h >= 2:
                    act.wait_ge(half_used, before + 2 * j + h - 1)
                nc.scalar.copy(w_hi[:, h], slot[j % MIX_SLOTS][:, h * HALF:(h + 1) * HALF]).then_inc(hi_ready, 1)

            def u_block(b):
                act.wait_ge(rinv_ready, 1)
                act.wait_ge(half_used, 2 * NB * (b + 1))
                nc.scalar.mul(u[:, 0, b * BLK:(b + 1) * BLK], bank[2 * (b % 2)][:, :], rinv[:, 0:1]).then_inc(u_out_act, 1)

            for b in range(NB):
                for g in range(NB):
                    for h in range(2):
                        high_part(b, g, h, 0)
                        if b == 0 and h == 0:
                            h_block(g)
                    if b == 1 and g < TC:
                        nc.scalar.activation(mid[:, g].rearrange("p h n -> p (h n)"), xs[:, g], ACT.Square,
                                             accum_out=ssq[:, g, 0:1]).then_inc(squares, 1)
                    if b == 1 and g == TC:
                        act.wait_ge(mean_ready, 1)
                        nc.scalar.activation(rms[:], rms[:], ACT.Sqrt).then_inc(root_ready, 1)
                        u_block(0)
                    if b >= 2 and g == 0:
                        u_block(b - 1)
            u_block(NB - 1)

            for h in range(HEADS):
                act.wait_ge(unit_done, U_AB + h + 1)
                nc.scalar.copy(ab[:, h], bank[h][:, :]).then_inc(unit_act, 1)
            for h in range(2):
                high_part(0, 0, h, HALVES)
            for h in range(HEADS):
                act.wait_ge(unit_done, U_PQ + h + 1)
                nc.scalar.copy(pq[:, h], bank[h][:, :]).then_inc(unit_act, 1)
            for g in range(POOL_GROUPS):
                act.wait_ge(unit_done, U_WP + g + 1)
                for e in range(HC):
                    m = g * HC + e
                    last = nc.scalar.mul(tr_hi[:, m], bank[4 + g][:, e * SEQ:(e + 1) * SEQ], pscale[:, m:m + 1])
                last.then_inc(unit_act, 1)
            for h in range(HEADS):
                act.wait_ge(unit_done, U_WF + h + 1)
                m = (POOL_GROUPS + h) * HC
                nc.scalar.copy(tr_hi[:, m:m + HC].rearrange("p c n -> p (c n)"), bank[h][:, :]).then_inc(unit_act, 1)

            def turned_block(b, chunks=range(TC)):
                for t in chunks:
                    act.wait_ge(x2_turned, TC * b + t + 1)
                    nc.scalar.copy(x2t[:, b % 2, :, t * P:(t + 1) * P],
                                   bank[4 + t][:, :].rearrange("p (k c) -> p k c", k=KPB)).then_inc(x2t_out, 1)

            def square_block(b, chunks=range(TC)):
                for t in chunks:
                    act.wait_ge(x2_out, TC * b + t + 1)
                    if b or t:
                        act.wait_ge(x2_squares, TC * b + t)
                    nc.scalar.activation(junk[:], xs[:, t, b * BLK:(b + 1) * BLK], ACT.Square,
                                         accum_out=ssq[:, t, b:b + 1]).then_inc(x2_squares, 1)
            for b in range(NB):
                for g in range(NB):
                    if b or g:
                        for h in range(2):
                            high_part(b, g, h, HALVES)
                    if b and g == 1:
                        turned_block(b - 1)
                    if b and g == 2:
                        square_block(b - 1)
            square_block(NB - 1, (0,))
            turned_block(NB - 1)
            square_block(NB - 1, (1,))

            act.wait_ge(exp_asked, 1)
            nc.scalar.activation(rms[:], rms[:], ACT.Sqrt).then_inc(exp_ready, 1)

            act.wait_ge(logits_done, 1)
            act.dma_start(gfin[:], g_final.unsqueeze(0).to_broadcast([P, D])).then_inc(gfin_in, 16)
            act.wait_ge(exp_asked, 2)
            nc.scalar.activation(exps[:], to_exp[:], ACT.Exp).then_inc(exp_ready, 1)

            act.wait_ge(rounds_ready, 1)
            more = act.value_load(rounds[0:1, 0:1], min_val=1, max_val=MAX_ROUNDS)

            def run_pair(pair, first, turn):
                for g in (1, 2, 3):
                    use = U_GATHER + g
                    act.wait_ge(swap_full, pair * SWAPS + use + 1)
                    for k in range(KPB):
                        kk = g * KPB + k
                        last = nc.scalar.mul(picked[:, kk], bank[6 + use % 2][:, k * P:(k + 1) * P], gffn[:, kk:kk + 1])
                    last.then_inc(swap_free[use % 2], 1)
                end = first + 4 * NB - 1
                act.wait_ge(slot_free[slot_of(end)], freed(end, turn))
                nc.scalar.activation(silu[:], bank[0][:, :], ACT.Silu).then_inc(silu_ready, 1)
                act.wait_ge(swap_full, pair * SWAPS + U_ACT + 1)
                nc.scalar.copy(act_cols[:].rearrange("p c n -> p (c n)"), bank[7][:, :]).then_inc(swap_free[1], 1)
                for n in range(NB):
                    end = first + 4 * NB + (n // 2 + 1) * FC - 1
                    act.wait_ge(slot_free[slot_of(end)], freed(end, turn))
                    nc.scalar.copy(expert_out[:, n * BLK:(n + 1) * BLK], bank[2 + n][:, :]).then_inc(down_out, 1)

            with act.Fori(0, more) as r:
                with act.Fori(0, TURNS) as q:
                    turn = r * TURNS + q
                    for i in range(TURN_PAIRS):
                        run_pair(turn * TURN_PAIRS + i, i * PAIR_SLABS, turn)

            nc.scalar.activation(junk[:, 0:TC], rms[:], ACT.Sqrt).then_inc(last_squares, 1)
            for i in range(3 * TC):
                t, n = i % TC, 1 + i // TC
                if n == 1:
                    act.wait_ge(pool_squares, TC + t + 1)
                    src, how = square_sum[:, t], ACT.Copy
                else:
                    act.wait_ge(swap_free[t], last_use(more, n))
                    src, how = xs[:, t, n * BLK:(n + 1) * BLK], ACT.Square
                act.wait_ge(last_squares, i + 1)
                nc.scalar.activation(junk[:], src, how, accum_out=ssq[:, t, n:n + 1]).then_inc(last_squares, 1)
            for t in range(TC):
                act.wait_ge(last_mean, t + 1)
                nc.scalar.activation(rms[:, t:t + 1], rms[:, t:t + 1], ACT.Sqrt).then_inc(last_root, 1)
            for t in range(TC):
                act.wait_ge(last_rinv, t + 1)
                act.wait_ge(scaled, 2 * TC)
                cols = slice(0, D // 2)
                nc.scalar.mul(u[:, t, cols], u[:, t, cols], rinv[:, t:t + 1]).then_inc(y_act, 1)

        @block.gpsimd
        def _(pool):
            pool.wait_ge(rounds_ready, 1)
            more = pool.value_load(rounds[0:1, 0:1], min_val=1, max_val=MAX_ROUNDS)
            pool.wait_ge(gfin_in, 16)
            for n in range(2):
                cols = slice(n * BLK, (n + 1) * BLK)
                for t in range(TC):
                    pool.wait_ge(swap_free[t], last_use(more, n))
                    if n == 0:
                        nc.gpsimd.tensor_tensor(square_sum[:, t], xs[:, t, cols], xs[:, t, cols], ALU.mult).then_inc(pool_squares, 1)
                        continue
                    if t:
                        pool.wait_ge(pool_squares, TC + t)
                    nc.gpsimd.tensor_tensor(block_squares, xs[:, t, cols], xs[:, t, cols], ALU.mult).then_inc(pool_block, 1)
                    pool.wait_ge(pool_block, t + 1)
                    pool.wait_ge(pool_squares, TC + t)
                    nc.gpsimd.tensor_tensor(square_sum[:, t], square_sum[:, t], block_squares, ALU.add).then_inc(pool_squares, 1)
            for t in range(TC):
                for n in range(2):
                    cols = slice(n * BLK, (n + 1) * BLK)
                    nc.gpsimd.tensor_tensor(u[:, t, cols], xs[:, t, cols], gfin[:, cols], ALU.mult).then_inc(scaled, 1)

        @block.vector
        def _(dve):
            dve.sem_inc(rank_moved, AHEAD)
            steps = [0]

            def link(instruction):
                steps[0] += 1
                instruction.then_inc(step, 1)
                dve.wait_ge(step, steps[0])

            def h_block(g):
                for k in range(KPB):
                    kk = g * KPB + k
                    dve.wait_ge(h_hi, (kk // 2 + 1) * 2)
                    src = bank[4 + (g % 2) * 2 + k // 2][:, (k % 2) * SEQ:(k % 2 + 1) * SEQ]
                    nc.vector.scalar_tensor_tensor(out=tr_lo[:, kk], in0=src, scalar=gmix[:, kk:kk + 1],
                                                   in1=tr_hi[:, kk].bitcast(f32), op0=ALU.mult,
                                                   op1=ALU.subtract).then_inc(h_lo, 1)

            def low_part(b, g, h, before):
                j = b * NB + g
                dve.wait_ge(hi_ready, before + 2 * j + h + 1)
                nc.vector.tensor_tensor(w_lo[:, h], slot[j % MIX_SLOTS][:, h * HALF:(h + 1) * HALF],
                                        w_hi[:, h].bitcast(f32), ALU.subtract).then_inc(lo_ready, 1)

            def u_block(b):
                dve.wait_ge(half_used, 2 * NB * (b + 1))
                nc.vector.tensor_scalar(u[:, 1, b * BLK:(b + 1) * BLK], bank[2 * (b % 2) + 1][:, :],
                                        rinv[:, 1:2], None, ALU.mult).then_inc(u_out, 1)

            dve.wait_ge(first_in, 16 * 2)
            for b in range(NB):
                for g in range(NB):
                    for h in range(2):
                        low_part(b, g, h, 0)
                        if b == 0 and h == 0:
                            h_block(g)
                    if b == 1 and g == TC - 1:
                        dve.wait_ge(squares, TC)
                        nc.vector.tensor_scalar(rms[:], ssq[:, :, 0], 1.0 / D, EPS, ALU.mult, ALU.add).then_inc(mean_ready, 1)
                    if b == 1 and g == TC:
                        dve.wait_ge(root_ready, 1)
                        nc.vector.reciprocal(rinv[:], rms[:]).then_inc(rinv_ready, 1)
                        dve.wait_ge(rinv_ready, 1)
                        u_block(0)
                    if b >= 2 and g == 0:
                        u_block(b - 1)
            u_block(NB - 1)
            dve.wait_ge(small_in, 16 * 6)
            nc.vector.memset(router_w[:, :, LOGITS:TILE], 0.0)
            for w, first, n in ((group_w, 0, GROUPS), (expert_w, GROUPS, EXPERTS)):
                last = nc.vector.tensor_tensor(router_w[:, :, first:first + n],
                                               w[:].rearrange("p g (k n) -> p (g k) n", n=n),
                                               gffn[:].unsqueeze(2).to_broadcast([P, KK, n]), ALU.mult)
            last.then_inc(router_scaled, 1)

            for h in range(2):
                low_part(0, 0, h, HALVES)
            for g in range(POOL_GROUPS):
                dve.wait_ge(unit_done, U_MEAN + g + 1)
                nc.vector.tensor_copy(pooled[:, g], bank[4 + g][:, :]).then_inc(unit_dve, 1)
            for h in range(HEADS):
                dve.wait_ge(unit_act, HEADS + h + 1)
                both = pq[:, h].rearrange("p (c n) -> p c n", c=HC)
                to = real[:, h].rearrange("p (c n) -> p c n", c=HC)
                mid_k = SEQ // 2
                nc.vector.tensor_copy(to[:, :, 0:mid_k + 1:mid_k], both[:, :, 0:mid_k + 1:mid_k])
                nc.vector.tensor_tensor(to[:, :, 1:mid_k], both[:, :, 1:mid_k], both[:, :, N_COS:SEQ], ALU.subtract)
                nc.vector.tensor_tensor(to[:, :, SEQ - 1:mid_k:-1], both[:, :, 1:mid_k], both[:, :, N_COS:SEQ],
                                        ALU.add).then_inc(unit_dve, 1)
            for g in range(POOL_GROUPS):
                dve.wait_ge(unit_act, 2 * HEADS + g + 1)
                for e in range(HC):
                    m = g * HC + e
                    last = nc.vector.scalar_tensor_tensor(out=tr_lo[:, m], in0=bank[4 + g][:, e * SEQ:(e + 1) * SEQ],
                                                          scalar=pscale[:, m:m + 1], in1=tr_hi[:, m].bitcast(f32),
                                                          op0=ALU.mult, op1=ALU.subtract)
                last.then_inc(unit_dve, 1)
            for h in range(HEADS):
                dve.wait_ge(unit_act, 3 * HEADS + h + 1)
                m = (POOL_GROUPS + h) * HC
                nc.vector.tensor_tensor(tr_lo[:, m:m + HC].rearrange("p c n -> p (c n)"), bank[h][:, :],
                                        tr_hi[:, m:m + HC].rearrange("p c n -> p (c n)").bitcast(f32),
                                        ALU.subtract).then_inc(unit_dve, 1)

            def x2_block(b):
                for t in range(TC):
                    if t == 0:
                        dve.wait_ge(first_chunk, b + 1)
                    else:
                        dve.wait_ge(half_used, HALVES + 2 * NB * (b + 1))
                    cols = xs[:, t, b * BLK:(b + 1) * BLK]
                    nc.vector.tensor_tensor(cols, bank[2 * (b % 2) + t][:, :], cols, ALU.add).then_inc(x2_out, 1)

            def snap_block(b):
                for t in range(TC):
                    dve.wait_ge(x2_out, TC * b + t + 1)
                    nc.vector.tensor_copy(snap[:, t, b * KPB:(b + 1) * KPB],
                                          xs[:, t, b * BLK:(b + 1) * BLK].rearrange("p (c k) -> p k c", k=KPB)).then_inc(snapped, 1)
            for b in range(NB):
                for g in range(NB):
                    if b or g:
                        for h in range(2):
                            low_part(b, g, h, HALVES)
                    if b and g == 0:
                        x2_block(b - 1)
                    if b and g == 1:
                        snap_block(b - 1)
            x2_block(NB - 1)
            snap_block(NB - 1)

            def wide(row, n):
                return row.unsqueeze(2).to_broadcast([P, TC, n])

            def first_max(values, n, row, mask, op=ALU.is_equal):
                idx = index[:, EXPERTS - n:]
                link(nc.vector.tensor_reduce(top[:, row], values, AX.X, ALU.max))
                for t in range(TC):
                    last = nc.vector.scalar_tensor_tensor(out=hit[:, t, 0:n], in0=values[:, t], scalar=top[:, row, t:t + 1],
                                                          in1=idx, op0=ALU.is_equal, op1=ALU.mult)
                link(last)
                link(nc.vector.tensor_reduce(top[:, 3], hit[:, :, 0:n], AX.X, ALU.min))
                link(nc.vector.tensor_tensor(mask, idx.unsqueeze(1).to_broadcast([P, TC, n]), wide(top[:, 3], n), op))

            dve.wait_ge(x2_squares, TC * NB)
            link(nc.vector.tensor_reduce(rms[:], ssq[:], AX.X, ALU.add))
            nc.vector.tensor_scalar(rms[:], rms[:], 1.0 / D, EPS, ALU.mult, ALU.add).then_inc(exp_asked, 1)
            dve.wait_ge(exp_ready, 1)
            link(nc.vector.reciprocal(rinv2[:], rms[:]))
            dve.wait_ge(tiles_done, 1)
            nc.vector.tensor_copy(tiles[:], bank[6][:, 0:SEQ]).then_inc(tiles_out, 1)
            dve.wait_ge(logits_done, 1)
            for t in range(TC):
                last = nc.vector.scalar_tensor_tensor(out=logit[:, t], in0=bank[7][:, t * LOGITS:(t + 1) * LOGITS],
                                                      scalar=rinv2[:, t:t + 1], in1=bias[:], op0=ALU.mult, op1=ALU.add)
            link(last)
            of_group, of_expert = logit[:, :, 0:GROUPS], logit[:, :, GROUPS:LOGITS]
            first_max(of_group, GROUPS, 0, other_group[:], ALU.not_equal)
            nc.vector.tensor_tensor(to_exp[:, :, 0:GROUPS], of_group, wide(top[:, 0], GROUPS), ALU.subtract)
            for t in range(TC):
                last = nc.vector.scalar_tensor_tensor(
                    out=masked[:, t].rearrange("p (g e) -> p g e", g=GROUPS),
                    in0=other_group[:, t].unsqueeze(2).to_broadcast([P, GROUPS, PER_GROUP]), scalar=-FAR,
                    in1=of_expert[:, t].rearrange("p (g e) -> p g e", g=GROUPS), op0=ALU.mult, op1=ALU.add)
            link(last)
            first_max(masked[:], EXPERTS, 1, best[:])
            link(nc.vector.scalar_tensor_tensor(out=masked2[:], in0=best[:], scalar=-2.0 * FAR, in1=masked[:],
                                                op0=ALU.mult, op1=ALU.add))
            first_max(masked2[:], EXPERTS, 2, second[:])
            nc.vector.tensor_tensor(to_exp[:, :, GROUPS], top[:, 2], top[:, 1], ALU.subtract).then_inc(exp_asked, 1)
            nc.vector.tensor_tensor(sel[:], best[:], second[:], ALU.add).then_inc(sel_ready, 1)
            dve.wait_ge(exp_ready, 2)
            link(nc.vector.tensor_reduce(share[:, 0], exps[:, :, 0:GROUPS], AX.X, ALU.add))
            link(nc.vector.tensor_scalar(share[:, 1], exps[:, :, GROUPS], 1.0, None, ALU.add))
            link(nc.vector.tensor_tensor(share[:, 0], share[:, 0], share[:, 1], ALU.mult))
            link(nc.vector.reciprocal(share[:, 2], share[:, 0]))
            link(nc.vector.tensor_tensor(share[:, 3], share[:, 2], exps[:, :, GROUPS], ALU.mult))
            link(nc.vector.tensor_tensor(best[:], best[:], wide(share[:, 2], EXPERTS), ALU.mult))
            link(nc.vector.tensor_tensor(second[:], second[:], wide(share[:, 3], EXPERTS), ALU.mult))
            link(nc.vector.tensor_tensor(comb[:, :, 0:EXPERTS], best[:], second[:], ALU.add))
            dve.wait_ge(ranks_done, 1)
            nc.vector.tensor_tensor(rank[:, :, 0:EXPERTS], bank[6][:, 0:2 * EXPERTS].rearrange("p (t e) -> p t e", t=TC),
                                    sel[:], ALU.mult)
            link(nc.vector.tensor_reduce(fullest[:], bank[6][:, 2 * EXPERTS:3 * EXPERTS], AX.X, ALU.max))
            nc.vector.tensor_copy(pair_rank[:], rank[:, :, 0:2])
            link(nc.vector.tensor_scalar(over[:, 0:MAX_ROUNDS - 1], bound, fullest[:, 0:1], None, ALU.is_lt))
            nc.vector.tensor_copy(pair_comb[:], comb[:, :, 0:2])
            link(nc.vector.tensor_reduce(over[:, MAX_ROUNDS - 1:MAX_ROUNDS], over[:, 0:MAX_ROUNDS - 1], AX.X, ALU.add))
            nc.vector.tensor_scalar(rounds[:], over[:, MAX_ROUNDS - 1:MAX_ROUNDS], 1.0, None, ALU.add).then_inc(rounds_ready, 1)

            def pair_matrices():
                for m in (pick, put):
                    for t in range(TC):
                        for e in range(2):
                            factor = rinv2[:, t:t + 1] if m is pick else pair_comb[:, t, e:e + 1]
                            last = nc.vector.tensor_scalar(m[:, t, e * CAP:(e + 1) * CAP], iota, pair_rank[:, t, e:e + 1],
                                                           factor, ALU.is_equal, ALU.mult)
                    if m is pick:
                        last.then_inc(pick_ready, 1)
                last.then_inc(put_ready, 1)

            pair_matrices()
            nc.vector.tensor_copy(comb[:, :, EXPERTS:], comb[:, :, 0:2])
            nc.vector.tensor_scalar(rank[:, :, EXPERTS:], rank[:, :, 0:2], -float(CAP), None, ALU.add)
            dve.wait_ge(rounds_ready, 1)
            more = dve.value_load(rounds[0:1, 0:1], min_val=1, max_val=MAX_ROUNDS)

            def run_pair(first, r, pair):
                dve.wait_ge(swap_full, pair * SWAPS + 1)
                nc.vector.tensor_tensor(picked[:, 0:KPB], bank[6][:, :].rearrange("p (k c) -> p k c", k=KPB),
                                        gffn[:, 0:KPB].unsqueeze(2).to_broadcast([P, KPB, 2 * CAP]),
                                        ALU.mult).then_inc(swap_free[0], 1)
                dve.wait_ge(swap_full, pair * SWAPS + U_PUT + 1)
                nc.vector.tensor_copy(put_t[:], bank[6][:, 0:SEQ]).then_inc(swap_free[0], 1)
                dve.wait_ge(rank_moved, AHEAD + r)
                nc.vector.tensor_copy(pair_rank[:], rank[:, :, bass.ds(first + 2, 2)])
                nc.vector.tensor_copy(pair_comb[:], comb[:, :, bass.ds(first + 2, 2)]).then_inc(pair_cols, 1)
                dve.wait_ge(pair_cols, pair + 1)
                pair_matrices()
                dve.wait_ge(silu_ready, pair + 1)
                nc.vector.tensor_tensor(act_rows[:], bank[1][:, :], silu[:], ALU.mult).then_inc(act_ready, 1)
                for i in range(2):
                    dve.wait_ge(swap_free[i], pair * (SWAPS // 2) + SWAPS // 2)
                for n in range(NB):
                    for t in range(TC):
                        use = U_SCATTER + n * TC + t
                        dve.wait_ge(swap_full, pair * SWAPS + use + 1)
                        cols = xs[:, t, n * BLK:(n + 1) * BLK]
                        nc.vector.tensor_tensor(cols, bank[6 + use % 2][:, :], cols, ALU.add).then_inc(swap_free[use % 2], 1)

            with dve.Fori(0, more) as r:
                with dve.Fori(0, TURNS) as q:
                    for i in range(TURN_PAIRS):
                        run_pair((q * TURN_PAIRS + i) * 2, r, (r * TURNS + q) * TURN_PAIRS + i)
                nc.vector.tensor_scalar(rank[:], rank[:], -float(CAP), None, ALU.add).then_inc(rank_moved, 1)

            for t in range(TC):
                dve.wait_ge(last_squares, 1 + 2 * TC + t + 1)
                link(nc.vector.tensor_reduce(rms[:, t:t + 1], ssq[:, t, 1:NB], AX.X, ALU.add))
                nc.vector.tensor_scalar(rms[:, t:t + 1], rms[:, t:t + 1], 1.0 / D, EPS, ALU.mult, ALU.add).then_inc(last_mean, 1)
            dve.wait_ge(gfin_in, 16)
            for i in range(2):
                dve.wait_ge(swap_free[i], last_use(more, NB - 1))
            for t in range(TC):
                dve.wait_ge(last_root, t + 1)
                nc.vector.reciprocal(rinv[:, t:t + 1], rms[:, t:t + 1]).then_inc(last_rinv, 1)
                dve.wait_ge(last_rinv, t + 1)
                cols = slice(D // 2, D)
                nc.vector.scalar_tensor_tensor(out=u[:, t, cols], in0=xs[:, t, cols], scalar=rinv[:, t:t + 1],
                                               in1=gfin[:, cols], op0=ALU.mult, op1=ALU.mult).then_inc(y_dve, 1)

def tables():
    consts = np.zeros((P, C_WIDTH), np.float32)
    consts[:, C_ID:C_ID + P] = np.eye(P)
    consts[:, C_TRI:C_TRI + P] = np.triu(np.ones((P, P)))
    consts[:, C_ONES:C_ONES + P] = 1.0
    consts[:, C_IOTA:C_IOTA + CAP] = np.arange(1, CAP + 1)
    consts[:, C_IDX:C_IDX + EXPERTS] = np.arange(EXPERTS) - EXPERTS
    consts[:, C_FULL:C_FULL + MAX_ROUNDS - 1] = CAP * np.arange(1, MAX_ROUNDS)
    for k in range(P // TILE):
        consts[k * TILE:k * TILE + LOGITS, C_SUM:] = np.eye(LOGITS)
    angle = 2.0 * np.pi / SEQ * (np.outer(np.arange(SEQ), np.arange(SEQ)) % SEQ)
    half = SEQ // 2
    dft_tokens = np.concatenate([np.cos(angle[:, :half + 1]), np.sin(angle[:, 1:half])], 1) / np.sqrt(SEQ)
    angle = 2.0 * np.pi / HD * (np.outer(np.arange(HD), np.arange(HD)) % HD)
    dft_channels = np.concatenate([np.cos(angle), np.sin(angle)], 0) / np.sqrt(HD)
    windows = []
    for k in WINDOWS:
        m = np.zeros((SEQ, SEQ))
        for t in range(SEQ):
            lo, hi = max(t - (k - 1) // 2, 0), min(t + k // 2 + 1, SEQ)
            m[lo:hi, t] = 1.0 / (hi - lo)
        windows.append(m - np.eye(SEQ))
    f = np.float32
    return {"consts": consts, "dft_tokens": dft_tokens.astype(f), "dft_channels": dft_channels.astype(f),
            "pool_windows": np.concatenate(windows, 0).astype(f)}


_INS = ["x", "g_mix", "w_in", "w_pool", "pool_scale", "w_fourier", "w_out", "g_ffn", "w_group_router",
        "b_group_router", "w_expert_router", "b_expert_router", "w_gate", "w_up", "w_down", "g_final"]


def kernel(**inputs):
    import concourse.bacc as bacc
    from concourse.bass_utils import run_bass_kernel_spmd

    nc = bacc.Bacc("TRN2", target_bir_lowering=False, num_devices=1)
    arrays, args = {}, []
    given = {n: np.ascontiguousarray(inputs[n]) for n in _INS}
    given["x"] = given["x"].reshape(SEQ, D)
    given.update(tables())
    for name, a in given.items():
        arrays[f"in_{name}"] = a
        args.append(nc.dram_tensor(f"in_{name}", a.shape, mybir.dt.from_np(a.dtype), kind="ExternalInput").ap())
    args.append(nc.dram_tensor("out_y", (SEQ, D), mybir.dt.float32, kind="ExternalOutput").ap())
    build(nc, *args)
    r = run_bass_kernel_spmd(nc, [arrays], core_ids=[0])
    return r.results[0]["out_y"].reshape(1, SEQ, D)
```
